# Optimizing a Trainium2 kernel written in Bass

```python
import jax, jax.numpy as jnp
from jax import lax
import numpy as np

D_MODEL = 2048
BATCH = 1
SEQ = 256
DEPTH = 1

HEAD_DIM = 128
N_HEADS_A = D_MODEL // (2 * HEAD_DIM)
N_KV_A = 2
N_HEADS_B = D_MODEL // (2 * HEAD_DIM)
N_KV_B = 2
N_HEADS = N_HEADS_A + N_HEADS_B
MIX_WIDTH = N_HEADS * HEAD_DIM
IDX_HEADS = 16
IDX_DIM = 64
TOPK_MAX = 256
WINDOW = 128
Q_BLOCK = 128
D_FF = 11 * D_MODEL // 4
CONV_WIDTH = 3
N_MOD = 6
EPS = 1e-6
NEG = -1e30
IN_WIDTH = (N_HEADS_A * HEAD_DIM + 2 * N_KV_A * HEAD_DIM + IDX_HEADS * IDX_DIM + IDX_DIM + IDX_HEADS
            + N_HEADS_B * HEAD_DIM + 2 * N_KV_B * HEAD_DIM)

kernel_name = "hymba_dsa_swa_sink_alibi_convffn_adaln"

def rms_norm(x, g):
    xf = x.astype(jnp.float32)
    y = xf * lax.rsqrt(jnp.mean(xf * xf, axis=-1, keepdims=True) + EPS)
    return (y * g.astype(jnp.float32)).astype(x.dtype)

def alibi_slopes(n):
    return 2.0 ** (-8.0 * jnp.arange(1, n + 1, dtype=jnp.float32) / n)

def split_sizes():
    return [N_HEADS_A * HEAD_DIM, N_KV_A * HEAD_DIM, N_KV_A * HEAD_DIM,
            IDX_HEADS * IDX_DIM, IDX_DIM, IDX_HEADS,
            N_HEADS_B * HEAD_DIM, N_KV_B * HEAD_DIM, N_KV_B * HEAD_DIM]

def dsa_attention(q, k, v, q_idx, k_idx, w_idx, slopes):
    B, S, H, dh = q.shape
    G = k.shape[2]
    R = H // G
    top_k = min(TOPK_MAX, S // 4)
    nb = S // Q_BLOCK
    key_pos = jnp.arange(S)
    scale = dh ** -0.5
    idx_scale = IDX_DIM ** -0.5
    slopes_gr = slopes.reshape(G, R)
    gather = jax.vmap(lambda a, i: a[i])

    def to_blocks(a):
        return jnp.moveaxis(a.reshape((B, nb, Q_BLOCK) + a.shape[2:]), 1, 0)

    def block(args):
        qb, qib, wb, start = args
        t = start + jnp.arange(Q_BLOCK)
        s_h = jnp.einsum('bqhd,bkd->bqhk', qib, k_idx, preferred_element_type=jnp.float32)
        score = jnp.einsum('bqhk,bqh->bqk', jax.nn.relu(s_h * idx_scale), wb.astype(jnp.float32))
        causal = key_pos[None, :] <= t[:, None]
        score = jnp.where(causal[None], score, NEG)
        _, sel = lax.top_k(score, top_k)
        valid = sel <= t[None, :, None]
        ks = gather(k, sel)
        vs = gather(v, sel)
        qg = qb.reshape(B, Q_BLOCK, G, R, dh)
        logits = jnp.einsum('bqgrd,bqkgd->bqgrk', qg, ks, preferred_element_type=jnp.float32) * scale
        dist = (t[None, :, None] - sel).astype(jnp.float32)
        logits = logits - slopes_gr[None, None, :, :, None] * dist[:, :, None, None, :]
        logits = jnp.where(valid[:, :, None, None, :], logits, NEG)
        p = jax.nn.softmax(logits, axis=-1).astype(v.dtype)
        o = jnp.einsum('bqgrk,bqkgd->bqgrd', p, vs)
        return o.reshape(B, Q_BLOCK, H * dh)

    starts = jnp.arange(nb, dtype=jnp.int32) * Q_BLOCK
    out = lax.map(block, (to_blocks(q), to_blocks(q_idx), to_blocks(w_idx), starts))
    return jnp.moveaxis(out, 0, 1).reshape(B, S, H * dh)

def swa_sink_attention(q, k, v, sinks, slopes):
    B, S, H, dh = q.shape
    G = k.shape[2]
    R = H // G
    nb = S // WINDOW
    qb = q.reshape(B, nb, WINDOW, G, R, dh)

    def band(a):
        a = a.reshape(B, nb, WINDOW, G, dh)
        prev = jnp.pad(a, ((0, 0), (1, 0), (0, 0), (0, 0), (0, 0)))[:, :-1]
        return jnp.concatenate([prev, a], axis=2)

    kb, vb = band(k), band(v)
    logits = jnp.einsum('bnqgrd,bnkgd->bngrqk', qb, kb, preferred_element_type=jnp.float32) * (dh ** -0.5)
    i = jnp.arange(WINDOW)[:, None]
    j = jnp.arange(2 * WINDOW)[None, :]
    dist = i + WINDOW - j
    key_abs = jnp.arange(nb)[:, None, None] * WINDOW - WINDOW + j[None]
    valid = (dist >= 0) & (dist < WINDOW) & (key_abs >= 0)
    logits = logits - slopes.reshape(G, R)[None, None, :, :, None, None] * dist.astype(jnp.float32)
    logits = jnp.where(valid[None, :, None, None], logits, NEG)
    sink = jnp.broadcast_to(sinks.astype(jnp.float32).reshape(1, 1, G, R, 1, 1), logits.shape[:-1] + (1,))
    p = jax.nn.softmax(jnp.concatenate([logits, sink], axis=-1), axis=-1)[..., :-1].astype(v.dtype)
    o = jnp.einsum('bngrqk,bnkgd->bnqgrd', p, vb)
    return o.reshape(B, S, H * dh)

def conv_gated_mlp(h, w_gate, w_up, conv_w, conv_b, w_down):
    g = h @ w_gate
    u = h @ w_up
    F = g.shape[-1]
    g = lax.conv_general_dilated(g, conv_w[:, None, :], window_strides=(1,),
                                 padding=[(CONV_WIDTH - 1, 0)],
                                 dimension_numbers=('NWC', 'WIO', 'NWC'),
                                 feature_group_count=F) + conv_b
    return (jax.nn.silu(g) * u) @ w_down

def setup_inputs(seed: int = 0) -> dict:
    key = jax.random.key(seed)
    ks = jax.random.split(key, 16)
    f32 = jnp.float32
    D = D_MODEL
    nrm = lambda k, shape, s: jax.random.normal(k, shape, f32) * s
    return {
        "x": nrm(ks[0], (BATCH, SEQ, D), 1.0),
        "c": nrm(ks[1], (BATCH, D), 1.0),
        "w_ada": nrm(ks[2], (DEPTH, D, N_MOD * D), 0.5 * D ** -0.5),
        "b_ada": nrm(ks[3], (DEPTH, N_MOD * D), 0.02),
        "g_mix": 1.0 + nrm(ks[4], (DEPTH, D), 0.02),
        "w_in": nrm(ks[5], (DEPTH, D, IN_WIDTH), D ** -0.5),
        "sinks": nrm(ks[6], (DEPTH, N_HEADS_B), 1.0),
        "w_o": nrm(ks[7], (DEPTH, MIX_WIDTH, D), MIX_WIDTH ** -0.5),
        "g_ffn": 1.0 + nrm(ks[8], (DEPTH, D), 0.02),
        "w_gate": nrm(ks[9], (DEPTH, D, D_FF), D ** -0.5),
        "w_up": nrm(ks[10], (DEPTH, D, D_FF), D ** -0.5),
        "conv_w": nrm(ks[11], (DEPTH, CONV_WIDTH, D_FF), CONV_WIDTH ** -0.5),
        "conv_b": nrm(ks[12], (DEPTH, D_FF), 0.02),
        "w_down": nrm(ks[13], (DEPTH, D_FF, D), D_FF ** -0.5),
        "g_final": 1.0 + nrm(ks[14], (D,), 0.02),
    }

def reference(x, c, w_ada, b_ada, g_mix, w_in, sinks, w_o, g_ffn, w_gate, w_up, conv_w, conv_b, w_down, g_final):
    B, S, _ = x.shape
    slopes = alibi_slopes(N_HEADS)
    slopes_a, slopes_b = slopes[0::2], slopes[1::2]
    sizes = split_sizes()
    split_points = [sum(sizes[:n]) for n in range(1, len(sizes))]
    for layer in range(DEPTH):
        mod = jax.nn.silu(c) @ w_ada[layer] + b_ada[layer]
        shift1, scale1, gate1, shift2, scale2, gate2 = jnp.split(mod[:, None, :], N_MOD, axis=-1)
        h = rms_norm(x, g_mix[layer]) * (1 + scale1) + shift1
        proj = h @ w_in[layer]
        qa, ka, va, qi, ki, wi, qb, kb, vb = jnp.split(proj, split_points, axis=-1)
        oa = dsa_attention(qa.reshape(B, S, N_HEADS_A, HEAD_DIM),
                           ka.reshape(B, S, N_KV_A, HEAD_DIM),
                           va.reshape(B, S, N_KV_A, HEAD_DIM),
                           qi.reshape(B, S, IDX_HEADS, IDX_DIM),
                           ki,
                           wi * (IDX_HEADS ** -0.5),
                           slopes_a)
        ob = swa_sink_attention(qb.reshape(B, S, N_HEADS_B, HEAD_DIM),
                                kb.reshape(B, S, N_KV_B, HEAD_DIM),
                                vb.reshape(B, S, N_KV_B, HEAD_DIM),
                                sinks[layer], slopes_b)
        mix = jnp.concatenate([oa, ob], axis=-1) @ w_o[layer]
        x = x + gate1 * mix
        h2 = rms_norm(x, g_ffn[layer]) * (1 + scale2) + shift2
        x = x + gate2 * conv_gated_mlp(h2, w_gate[layer], w_up[layer], conv_w[layer], conv_b[layer], w_down[layer])
    return rms_norm(x, g_final)


_drawn_inputs = setup_inputs


def setup_inputs(seed=0):
    import zlib

    import numpy as np

    out = dict(_drawn_inputs(seed))
    spreads = {}
    factors = {'g_mix': 3.582, 'sinks': 8.372, 'g_ffn': 8.0, 'conv_b': 23.875, 'g_final': 7.625}
    for name, (base, spread) in spreads.items():
        noise = np.random.default_rng([zlib.crc32(name.encode()), seed]).standard_normal(out[name].shape)
        drawn = base * np.exp(spread * noise) if base else spread * noise
        out[name] = __import__('jax').numpy.asarray(drawn.astype(out[name].dtype))
    for name, factor in factors.items():
        out[name] = (out[name] * factor).astype(out[name].dtype)
    return out
```

```python
from contextlib import ExitStack

import concourse.bass as bass
from concourse import mybir

ALU = mybir.AluOpType
ACT = mybir.ActivationFunctionType
AX = mybir.AxisListType
F32 = mybir.dt.float32
F32R = mybir.dt.float32r

P = 128
D = 2048
S = 256
HD = 128
KT = D // P
NB = S // P
HEADS = 8
KV = 2
IDXH = 16
IDXD = 64
TOPK = min(256, S // 4)
WINDOW = 128
F = 11 * D // 4
FT = F // P
EPS = 1e-6
NEG = -1e30
TAKEN = -3e38
NQ = 4
QT = KT // NQ
CW = 512
CT = CW // P
RAW = 4
PAIR = 4
PASSES = F // CW
SMALL = IDXD + IDXH
IN_W = 2 * (HEADS + 2 * KV) * HD + IDXH * IDXD + SMALL
T_QA, T_KA, T_VA, T_QI, T_KI, T_QB, T_KB, T_VB = 0, 8, 10, 12, 20, 21, 29, 31
NT = 33
TILE_ORDER = [0, 2, 1, 3]
WIN_COL = [0, 512, 1024, 1536, 2048, 2640, 3152, 3664]
WIN_TILE = [0, 4, 8, 12, 16, 21, 25, 29]
SMALL_COL = 2560
NWIN = len(WIN_COL)
SLOPE = [2.0 ** (-8.0 * (n + 1) / (2 * HEADS)) for n in range(2 * HEADS)]
SHIFT1, SCALE1, GATE1, SHIFT2, SCALE2, GATE2 = range(6)

SEG_ADA0 = ("A" * 8, 1)
SEG_IN = ("AW" * 8, 3)
SEG_IN3 = ("AW" * 8, 1)
SEG_MID = ("A" * 8 + "P" * 16 + "WPP" * 8 + "W" * 8, 1)
SEG_UP0 = ("W" * 8, 1)
SEG_FFN_A = ("WWWAWWWAWWWAWWWA", 4)
SEG_FFN = ("W" * 12, 6)
SEG_LAST = ("W" * 4, 1)
SEGS = [SEG_ADA0, SEG_IN, SEG_IN3, SEG_MID, SEG_UP0, SEG_FFN_A, SEG_FFN, SEG_LAST]


def later(n):
    return not (isinstance(n, int) and n == 0)


class Stream:

    def __init__(self, index):
        self.kinds, self.times = SEGS[index]
        self.before = {k: sum(s.count(k) * t for s, t in SEGS[:index]) for k in "AWP"}
        self.start = sum(len(s) * t for s, t in SEGS[:index])

    def number(self, j, i=0):
        return self.start + i * len(self.kinds) + j

    def slot(self, j):
        return (self.start + j) % RAW

    def loads(self, j, i=0):
        return (self.start + j) // RAW + 1 + i * (len(self.kinds) // RAW)

    def of_kind(self, k, j, i=0):
        return self.before[k] + i * self.kinds.count(k) + self.kinds[:j + 1].count(k)

    def pair(self, j):
        return (self.of_kind("W", j) - 1) % PAIR

    def js(self, k):
        return [j for j, x in enumerate(self.kinds) if x == k]


ADA0, IN, IN3, MID, UP0, FFN_A, FFN, LAST = (Stream(n) for n in range(len(SEGS)))


def program(nc, x, c, w_ada, b_ada, g_mix, w_in, sinks, w_o, g_ffn, w_gate, w_up, conv_w, conv_b,
            w_down, g_final, out):
    ctx = ExitStack()
    with ctx:
        def sb(name, shape, dt=F32):
            return ctx.enter_context(nc.sbuf_tensor(name, shape, dt))

        def sem(name):
            return ctx.enter_context(nc.semaphore(name))

        x_sb = sb("x_sb", [P, NB, D])
        op_hi = sb("op_hi", [P, KT, S], F32R)
        op_lo = sb("op_lo", [P, KT, S], F32R)
        raw = sb("raw", [P, RAW, 2048])
        pair_hi = [None] * PAIR
        pair_lo = [None] * PAIR
        for n in range(2):
            pair_hi[n] = sb(f"pair_hi{n}", [P, 2048], F32R)
            pair_lo[n] = sb(f"pair_lo{n}", [P, 2048], F32R)
        h32 = sb("h32", [P, QT, S])
        xn = sb("xn", [P, NB, CW])
        ada_acc = sb("ada_acc", [P, 2, CW])
        with nc.sbuf_tensor("rows", [44, 7, P], F32) as rows:
            pass
        gate_row = sb("gate_row", [P, D])
        ki_raw = sb("ki_raw", [P, QT, SMALL])
        ki_hi = sb("ki_hi", [P, QT, SMALL], F32R)
        ki_lo = sb("ki_lo", [P, QT, SMALL], F32R)
        ident = sb("ident", [P, P])
        ones = sb("ones", [P, P])
        b_rows = sb("b_rows", [24, CW])
        cols = sb("cols", [P, 7, 44])
        silu_c = sb("silu_c", [P, KT])
        mod_s = sb("mod_s", [P, KT])
        mod_b = sb("mod_b", [P, KT])
        sink_row = sb("sink_row", [P, HEADS])
        stat = sb("stat", [P, 8])

        with ExitStack() as att:
            def sba(name, shape, dt=F32):
                return att.enter_context(nc.sbuf_tensor(name, shape, dt))
            logit = sba("logit", [P, 2, 4, S])
            probT = sba("probT", [P, 2, 4 * P])
            v_tok = sba("v_tok", [P, NB, 4, HD])
            score = sba("score", [P, NB, S])
            w_tok = sba("w_tok", [P, NB, P])
            bias = sba("bias", [P, 2, S])
            dist = sba("dist", [P, 3 * P])
            mask_c = sba("mask_c", [P, 3 * P])
            mask_w = sba("mask_w", [P, 3 * P])
            mask_a = sba("mask_a", [P, 3 * P])
            top8 = sba("top8", [P, 8])
            mx = sba("mx", [P, 2, 4])
            nmx = sba("nmx", [P, 2, 4])
            den = sba("den", [P, 2, 4])
            sink_e = sba("sink_e", [P, 2, 4])
            sink_d = sba("sink_d", [P, 2, 4])
            rden = sba("rden", [P, 2, 4])
            ki_dup = sba("ki_dup", [P, S])
        for n in range(2, PAIR):
            pair_hi[n] = sb(f"pair_hi{n}", [P, 2048], F32R)
            pair_lo[n] = sb(f"pair_lo{n}", [P, 2048], F32R)
        with ExitStack() as ffn:
            def sbf(name, shape, dt=F32):
                return ffn.enter_context(nc.sbuf_tensor(name, shape, dt))
            act_hi = sbf("act_hi", [P, CT, S], F32R)
            act_lo = sbf("act_lo", [P, CT, S], F32R)
            conv = sbf("conv", [P, CT, S])
            y = sbf("y", [P, NB, D])
        proj = sb("proj", [P, NT, S])

        ps = ctx.enter_context(nc.psum_tensor("ps", [P, 8, 512], F32))

        raw_in = [sem(f"raw_in{n}") for n in range(RAW)]
        ada_sum = sem("ada_sum")
        w_split = sem("w_split")
        p_used = sem("p_used")
        w_hi = sem("w_hi")
        w_used = sem("w_used")
        x_in = sem("x_in")
        c_in = sem("c_in")
        rows_in = sem("rows_in")
        sink_in = sem("sink_in")
        const_ready = sem("const_ready")
        masks_ready = sem("masks_ready")
        c_act = sem("c_act")
        cols_ps = sem("cols_ps")
        cols_ready = sem("cols_ready")
        sq_done = sem("sq_done")
        var_done = sem("var_done")
        root_done = sem("root_done")
        rstd_done = sem("rstd_done")
        xn_ready = sem("xn_ready")
        xnT_ready = sem("xnT_ready")
        mod_ps = sem("mod_ps")
        mod_done = sem("mod_done")
        h_ready = sem("h_ready")
        h_hi = sem("h_hi")
        h_lo = sem("h_lo")
        ki_in = sem("ki_in")
        ki_hi_done = sem("ki_hi_done")
        ki_split = sem("ki_split")
        ki_used = sem("ki_used")
        win_added = sem("win_added")
        ki_added = sem("ki_added")
        proj_zero = sem("proj_zero")
        gate_ps = sem("gate_ps")
        gate_done = sem("gate_done")
        q_scaled = sem("q_scaled")
        dup_in = sem("dup_in")
        vT_ps = sem("vT_ps")
        v_ready = sem("v_ready")
        idx_ps = sem("idx_ps")
        idx_relu = sem("idx_relu")
        idx_sum = sem("idx_sum")
        lg_ps = sem("lg_ps")
        lg_done = sem("lg_done")
        e_done = sem("e_done")
        p_ready = sem("p_ready")
        pT_ps = sem("pT_ps")
        pT_ready = sem("pT_ready")
        o_ps = sem("o_ps")
        o_hi = sem("o_hi")
        o_lo = sem("o_lo")
        mix_step = sem("mix_step")
        mod2_ps = sem("mod2_ps")
        mod2_done = sem("mod2_done")
        y_zero = sem("y_zero")
        conv_a = sem("conv_a")
        conv_step = sem("conv_step")
        silu_done = sem("silu_done")
        gu_done = sem("gu_done")
        act_hi_done = sem("act_hi_done")
        act_split = sem("act_split")
        y_added = sem("y_added")
        gate2_ps = sem("gate2_ps")
        x_step = sem("x_step")
        gf_in = sem("gf_in")
        y_ready = sem("y_ready")
        out_done = sem("out_done")
        chain = sem("chain")

        C_C, C_GM, C_GF, C_W0, C_W1, C_W2, C_B = range(7)

        def in_chunk(q, w):
            return w_in[0, bass.ds(q * CW, CW), WIN_COL[w]:WIN_COL[w] + CW]

        def quarter(ap):
            return ap.rearrange("(k p) n -> p k n", p=P)

        def used(seg, count):
            return PAIR + count + (2 if seg in (FFN_A, FFN, LAST) else 0)

        UP_END = PAIR + UP0.of_kind("W", 7)

        def split(count):
            return count + 1

        block = ctx.enter_context(nc.Block())

        @block.sync
        def _(sp):
            segs = [ADA0, IN, IN3, MID, UP0, FFN_A, FFN, LAST]

            def load(seg, j, i, src, tiles=QT):
                waits = []
                if seg is not ADA0 or j >= RAW:
                    if j >= RAW:
                        need = {seg.kinds[j - RAW]: seg.of_kind(seg.kinds[j - RAW], j - RAW, i)}
                    else:
                        ends = [segs[segs.index(seg) - 1].kinds] + [seg.kinds] * (seg.times > 1)
                        need = {}
                        for kind in {end[j - RAW] for end in ends}:
                            after = min(end[len(end) + j - RAW + 1:].count(kind) for end in ends)
                            count = seg.before[kind] - after
                            need[kind] = max(count, 0) + i * seg.kinds.count(kind)
                    for kind, count in need.items():
                        what, count = {"A": (ada_sum, count * QT), "W": (w_split, split(count)),
                                       "P": (p_used, count)}[kind]
                        waits.append((what, sp.lower_val(count)))
                if len(waits) == 2:
                    sp.wait_ge(*waits[1])
                dma = sp.dma_start(raw[:, seg.slot(j), :].rearrange("p (k n) -> p k n", k=tiles), src)
                dma.then_inc(raw_in[seg.slot(j)], 16)
                if waits:
                    dma.wait_op(*waits[0], "sem-ge")


            def ada(which, q, k):
                return quarter(w_ada[0, k * CW:(k + 1) * CW, bass.ds(which * D + q * CW, CW)])

            sp.dma_start(ki_raw[:, :, :], quarter(w_in[0, 0:CW, SMALL_COL:SMALL_COL + SMALL]))\
                .then_inc(ki_in, 16)
            for j in range(8):
                load(ADA0, j, 0, ada((SCALE1, SHIFT1)[j // 4], 0, j % 4))
            with sp.Fori(0, 3) as q:
                for w in range(NWIN):
                    load(IN, 2 * w, q, ada((SCALE1, SHIFT1)[w // 4], q + 1, w % 4))
                    load(IN, 2 * w + 1, q, quarter(in_chunk(q, w)))
                sp.wait_ge(ki_split, q + 1)
                sp.wait_ge(ki_in, 16)
                sp.dma_start(ki_raw[:, :, :],
                             quarter(w_in[0, bass.ds((q + 1) * CW, CW), SMALL_COL:SMALL_COL + SMALL]))\
                    .then_inc(ki_in, 16)
            for w in range(NWIN):
                load(IN3, 2 * w, 0, ada(GATE1, w // 4, w % 4))
                load(IN3, 2 * w + 1, 0, quarter(in_chunk(3, w)))
            mid = iter([ada(GATE1, 2 + n // 4, n % 4) for n in range(8)])
            mod2 = iter([ada((SCALE2, SHIFT2)[n // 16], (n // 4) % 4, n % 4) for n in range(32)])
            wo = iter([w_o[0, n * 2 * P:(n + 1) * 2 * P, h * 1024:(h + 1) * 1024]
                       .rearrange("(k p) n -> p k n", p=P) for h in range(2) for n in range(8)])
            for j, kind in enumerate(MID.kinds):
                load(MID, j, 0, next({"A": mid, "P": mod2, "W": wo}[kind]), 2 if kind == "W" else QT)

            def up(g, n):
                w = (w_gate, w_up)[n % 2]
                return quarter(w[0, (n // 2) * CW:(n // 2 + 1) * CW, bass.ds(g * CW, CW)])

            def down(g, n):
                return w_down[0, bass.ds(g * CW + (n % 2) * 2 * P, 2 * P),
                              (n // 2) * 1024:(n // 2 + 1) * 1024].rearrange("(k p) n -> p k n", p=P)

            def ffn_body(seg, i, g):
                ws = iter([(up(g, n), QT) for n in range(4)] + [(down(g - 1, n), 2) for n in range(2)]
                          + [(up(g, n), QT) for n in range(4, 8)] + [(down(g - 1, n), 2) for n in range(2, 4)])
                a = 0
                for j, kind in enumerate(seg.kinds):
                    if kind == "A":
                        load(seg, j, i, ada(GATE2, i, a))
                        a += 1
                    else:
                        src, tiles = next(ws)
                        load(seg, j, i, src, tiles)

            for n in range(8):
                load(UP0, n, 0, up(0, n))
            with sp.Fori(0, FFN_A.times) as i:
                ffn_body(FFN_A, i, i + 1)
            with sp.Fori(0, FFN.times) as i:
                ffn_body(FFN, i, i + 1 + FFN_A.times)
            for n in range(4):
                load(LAST, n, 0, down(PASSES - 1, n), 2)
            sp.wait_ge(w_split, split(LAST.of_kind("W", 3)))
            sp.dma_start(raw[:, 0, :], g_final[None, :].to_broadcast([P, D])).then_inc(gf_in, 16)
            for b in range(NB):
                sp.wait_ge(y_ready, b + 1)
                sp.dma_start(out[0, b * P:(b + 1) * P, :], raw[:, 2 + b, :]).then_inc(out_done, 16)
            sp.wait_ge(out_done, 16 * NB)

        @block.gpsimd
        def _(pool):
            nc.gpsimd.memset(ident[:, :], 0.0).then_inc(const_ready, 1)
            nc.gpsimd.memset(ones[:, :], 1.0).then_inc(const_ready, 1)
            nc.gpsimd.memset(rows[:, :, :], 0.0).then_inc(const_ready, 1)
            pool.wait_ge(const_ready, 3)
            nc.gpsimd.affine_select(out=ident[:, :], in_=ident[:, :], compare_op=ALU.not_equal, fill=1.0,
                                    base=0, pattern=[[-1, P]], channel_multiplier=1).then_inc(const_ready, 1)
            nc.gpsimd.memset(proj[:, :, :], 0.0).then_inc(proj_zero, 1)
            pool.wait_ge(w_used, used(IN3, IN3.of_kind("W", 15)))
            nc.gpsimd.iota(dist[:, 0:P], pattern=[[-1, P]], base=0, channel_multiplier=1,
                           allow_small_or_imprecise_dtypes=True)
            nc.gpsimd.iota(dist[:, P:3 * P], pattern=[[-1, S]], base=P, channel_multiplier=1,
                           allow_small_or_imprecise_dtypes=True).then_inc(masks_ready, 1)
            nc.gpsimd.memset(mask_c[:, :], 0.0).then_inc(masks_ready, 1)
            pool.wait_ge(masks_ready, 2)
            nc.gpsimd.affine_select(out=mask_c[:, 0:P], in_=mask_c[:, 0:P], compare_op=ALU.is_ge, fill=NEG,
                                    base=0, pattern=[[-1, P]], channel_multiplier=1).then_inc(masks_ready, 1)
            nc.gpsimd.affine_select(out=mask_c[:, P:3 * P], in_=mask_c[:, P:3 * P], compare_op=ALU.is_ge,
                                    fill=NEG, base=P, pattern=[[-1, S]], channel_multiplier=1)\
                .then_inc(masks_ready, 1)
            pool.wait_ge(masks_ready, 4)
            nc.gpsimd.tensor_copy(mask_w[:, 0:P], mask_c[:, 0:P]).then_inc(masks_ready, 1)
            nc.gpsimd.affine_select(out=mask_w[:, P:3 * P], in_=mask_c[:, P:3 * P], compare_op=ALU.is_ge,
                                    fill=NEG, base=WINDOW - 1 - P, pattern=[[1, S]], channel_multiplier=-1)\
                .then_inc(masks_ready, 1)
            pool.wait_ge(o_lo, 8)
            nc.gpsimd.memset(y[:, :, :], 0.0).then_inc(y_zero, 1)

        @block.scalar
        def _(act):
            def split_hi(seg, j, i=0):
                m = seg.of_kind("W", j, i)
                act.wait_ge(raw_in[seg.slot(j)], 16 * seg.loads(j, i))
                act.wait_ge(w_used, used(seg, m - PAIR))
                nc.scalar.copy(pair_hi[seg.pair(j)][:, :], raw[:, seg.slot(j), :]).then_inc(w_hi, 1)

            def split_ki(q):
                act.wait_ge(ki_in, 16 * (q + 1))
                nc.scalar.copy(ki_hi[:, :, :], ki_raw[:, :, :]).then_inc(ki_hi_done, 1)

            def squares(n):
                for b in range(NB):
                    ins = nc.scalar.activation(ps[:, 4 * b:4 * b + 4, :].rearrange("p a n -> p (a n)"),
                                               x_sb[:, b, :], ACT.Square,
                                               accum_out=stat[:, b:b + 1]).then_inc(sq_done, 1)
                act.wait_ge(var_done, n + 1)
                nc.scalar.activation(stat[:, 4:6], stat[:, 2:4], ACT.Sqrt).then_inc(root_done, 1)

            def normalise(q, n, norm):
                act.wait_ge(rstd_done, norm + 1)
                if later(n):
                    act.wait_ge(xnT_ready, n)
                for b in range(NB):
                    ins = nc.scalar.activation(xn[:, b, :], x_sb[:, b, bass.ds(q * CW, CW)], ACT.Copy,
                                               scale=stat[:, 6 + b:7 + b])
                ins.then_inc(xn_ready, 1)

            act.wait_ge(const_ready, 4)
            act.dma_start(rows[0:KT, C_C, :], c[0, :].rearrange("(k p) -> k p", p=P)).then_inc(c_in, 16)
            for b in range(NB):
                act.dma_start(x_sb[:, b, :], x[0, b * P:(b + 1) * P, :]).then_inc(x_in, 16)
            act.dma_start(rows[0:KT, C_GM, :], g_mix[0, :].rearrange("(k p) -> k p", p=P)).then_inc(rows_in, 16)
            act.dma_start(rows[0:KT, C_GF, :], g_ffn[0, :].rearrange("(k p) -> k p", p=P)).then_inc(rows_in, 16)
            for n in range(3):
                act.dma_start(rows[0:FT, C_W0 + n, :], conv_w[0, n, :].rearrange("(k p) -> k p", p=P))\
                    .then_inc(rows_in, 16)
            act.dma_start(rows[0:FT, C_B, :], conv_b[0, :].rearrange("(k p) -> k p", p=P)).then_inc(rows_in, 16)
            act.dma_start(b_rows[:, :], b_ada[0, :].rearrange("(k p) -> k p", p=CW)).then_inc(rows_in, 16)
            act.dma_start(sink_row[:, :], sinks[0:1, :].to_broadcast([P, HEADS])).then_inc(sink_in, 16)
            act.wait_ge(c_in, 16)
            nc.scalar.activation(rows[0:KT, C_C, :], rows[0:KT, C_C, :], ACT.Silu).then_inc(c_act, 1)
            act.wait_ge(x_in, 16 * NB)
            squares(0)
            normalise(0, 0, 0)
            act.wait_ge(h_ready, 1)
            nc.scalar.copy(op_hi[:, 0:QT, :], h32[:, :, :]).then_inc(h_hi, 1)

            def in_phase(seg, i, q):
                for w in range(NWIN):
                    split_hi(seg, 2 * w + 1, i)
                    if w == 1:
                        split_ki(q)
                    if w == 2 and seg is IN:
                        normalise(q + 1, q + 1, 0)
                if seg is IN:
                    act.wait_ge(h_ready, q + 2)
                    act.wait_ge(w_used, used(IN, NWIN * (q + 1)))
                    act.wait_ge(ki_used, q + 1)
                    nc.scalar.copy(op_hi[:, 0:QT, :], h32[:, :, :]).then_inc(h_hi, 1)

            with act.Fori(0, 3) as q:
                in_phase(IN, q, q)
            in_phase(IN3, 0, 3)

            def gate(n):
                act.wait_ge(gate_ps, n + 1)
                nc.scalar.copy(gate_row[:, n * CW:(n + 1) * CW], ps[:, 7, :]).then_inc(gate_done, 1)

            gate(0)
            act.wait_ge(ki_added, NQ)
            act.wait_ge(win_added, NQ * NWIN + 1)
            act.dma_start(ki_dup[IDXD:2 * IDXD, :], proj[0:IDXD, T_KI, :]).then_inc(dup_in, 16)
            gate(1)
            for t in (T_QB, T_QA):
                nc.scalar.mul(proj[:, t:t + HEADS, :], proj[:, t:t + HEADS, :], HD ** -0.5)\
                    .then_inc(q_scaled, 1)
            for n in range(8):
                act.wait_ge(idx_ps, n + 1)
                if n >= 2:
                    act.wait_ge(idx_sum, 4 * (n - 1))
                w = P * (n // 4 + 1)
                s = n % 2
                nc.scalar.activation(logit[:, s, :, 0:w],
                                     ps[:, 2 * s:2 * s + 2, :].rearrange("p a (h k) -> p (a h) k", h=2)[:, :, 0:w],
                                     ACT.Relu).then_inc(idx_relu, 1)
                if n == 3:
                    gate(2)
                if n == 7:
                    gate(3)

            def exps(u):
                g, b = divmod(u, NB)
                w = P * (b + 1)
                act.wait_ge(lg_done, u + 1)
                for r in range(4):
                    ins = nc.scalar.activation(logit[:, u % 2, r, 0:w], logit[:, u % 2, r, 0:w], ACT.Exp,
                                               bias=nmx[:, u % 2, r:r + 1], accum_out=den[:, u % 2, r:r + 1])
                if g < KV:
                    ins = nc.scalar.activation(sink_e[:, u % 2, :], sink_d[:, u % 2, :], ACT.Exp)
                ins.then_inc(e_done, 1)

            def outputs(u):
                g, b = divmod(u, NB)
                act.wait_ge(pT_ps, u + 1)
                if u:
                    act.wait_ge(o_ps, u)
                nc.scalar.copy(probT[:, 0:b + 1, :], ps[:, 4:5 + b, :]).then_inc(pT_ready, 1)
                act.wait_ge(o_ps, u + 1)
                t = (HEADS if g < KV else 0) + 4 * (g % KV)
                nc.scalar.copy(op_hi[:, t:t + 4, b * P:(b + 1) * P],
                               ps[:, 6, :].rearrange("p (h q) -> p h q", h=4)).then_inc(o_hi, 1)

            exps(0)
            for u in range(8):
                if u < 7:
                    exps(u + 1)
                outputs(u)
            for j in MID.js("W"):
                split_hi(MID, j)

            act.wait_ge(mix_step, 8)
            squares(1)

            def second(q):
                act.wait_ge(h_ready, NQ + q + 1)
                nc.scalar.copy(op_hi[:, QT * q:QT * q + QT, :], h32[:, :, :]).then_inc(h_hi, 1)

            normalise(0, NQ, 1)
            for q in range(NQ):
                if q < NQ - 1:
                    normalise(q + 1, NQ + q + 1, 1)
                second(q)
                split_hi(UP0, 2 * q)
                split_hi(UP0, 2 * q + 1)

            def conv_tail(g):
                for n, t in enumerate(TILE_ORDER):
                    if n == 0:
                        act.wait_ge(w_used, UP_END + 12 * g)
                    if n >= 2:
                        act.wait_ge(conv_step, 2 * CT * g + 2 * (n - 1))
                    nc.scalar.activation(conv[:, t, :], ps[:, t // 2, (t % 2) * S:(t % 2) * S + S], ACT.Identity,
                                         bias=cols[:, C_B, bass.ds(g * CT + t, 1)],
                                         scale=cols[:, C_W2, bass.ds(g * CT + t, 1)]).then_inc(conv_a, 1)
                act.wait_ge(conv_step, 2 * CT * (g + 1))
                nc.scalar.activation(conv[:, :, :], conv[:, :, :], ACT.Silu).then_inc(silu_done, 1)
                act.wait_ge(gu_done, g + 1)
                act.wait_ge(w_used, UP_END + 2 + 12 * g)
                nc.scalar.copy(act_hi[:, :, :], conv[:, :, :]).then_inc(act_hi_done, 1)

            def ffn_body(seg, i, g):
                for n, j in enumerate(seg.js("W")):
                    split_hi(seg, j, i)
                    if n == 1:
                        conv_tail(g - 1)

            with act.Fori(0, FFN_A.times) as i:
                ffn_body(FFN_A, i, i + 1)
            with act.Fori(0, FFN.times) as i:
                ffn_body(FFN, i, i + 1 + FFN_A.times)
            split_hi(LAST, 0)
            split_hi(LAST, 1)
            conv_tail(PASSES - 1)
            split_hi(LAST, 2)
            split_hi(LAST, 3)
            act.wait_ge(x_step, 2 * NB)
            squares(2)

        @block.vector
        def _(dve):
            chained = [0]

            def link(ins):
                chained[0] += 1
                ins.then_inc(chain, 1)
                dve.wait_ge(chain, chained[0])

            def split_lo(seg, j, i=0):
                dve.wait_ge(w_hi, seg.of_kind("W", j, i))
                nc.vector.tensor_tensor(pair_lo[seg.pair(j)][:, :], raw[:, seg.slot(j), :],
                                        pair_hi[seg.pair(j)][:, :].bitcast(F32), ALU.subtract).then_inc(w_split, 1)

            def add_ada(seg, j, i, acc, k):
                n = seg.of_kind("A", j, i)
                dve.wait_ge(raw_in[seg.slot(j)], 16 * seg.loads(j, i))
                for t in range(QT):
                    w = raw[:, seg.slot(j), t * CW:(t + 1) * CW]
                    col = silu_c[:, k * QT + t:k * QT + t + 1]
                    if k == 0 and t == 0:
                        ins = nc.vector.tensor_scalar(acc, w, col, None, ALU.mult)
                    else:
                        dve.wait_ge(ada_sum, (n - 1) * QT + t)
                        ins = nc.vector.scalar_tensor_tensor(acc, w, col, acc, ALU.mult, ALU.add)
                    ins.then_inc(ada_sum, 1)

            dve.wait_ge(cols_ps, 1)
            nc.vector.tensor_copy(silu_c[:, :], ps[:, 7, 0:KT]).then_inc(cols_ready, 1)
            def rms(n):
                dve.wait_ge(sq_done, NB * (n + 1))
                nc.vector.tensor_scalar(stat[:, 2:4], stat[:, 0:2], 1.0 / D, EPS, ALU.mult, ALU.add)\
                    .then_inc(var_done, 1)
                dve.wait_ge(root_done, n + 1)
                nc.vector.reciprocal(stat[:, 6:8], stat[:, 4:6]).then_inc(rstd_done, 1)

            rms(0)
            dve.sem_inc(w_split, 1)
            dve.wait_ge(cols_ps, 2)
            nc.vector.tensor_copy(cols[:, 1:7, :], ps[:, 6, 0:6 * 44].rearrange("p (a n) -> p a n", a=6))\
                .then_inc(cols_ready, 1)
            dve.wait_ge(cols_ready, 2)

            def mod_columns(q, g_col, n):
                dve.wait_ge(mod_ps, n + 1)
                nc.vector.scalar_tensor_tensor(mod_s[:, bass.ds(q * QT, QT)], ps[:, 7, 0:QT], 1.0,
                                               cols[:, g_col, bass.ds(q * QT, QT)], ALU.add, ALU.mult)\
                    .then_inc(mod_done, 1)
                nc.vector.tensor_copy(mod_b[:, bass.ds(q * QT, QT)], ps[:, 7, QT:2 * QT]).then_inc(mod_done, 1)
                dve.wait_ge(mod_done, 2 * n + 2)

            def modulate(q, n, tile, free_after=None):
                dve.wait_ge(xnT_ready, n + 1)
                if later(n):
                    dve.wait_ge(h_lo, n)
                for t in range(QT):
                    ins = nc.vector.tensor_scalar(h32[:, t, :], ps[:, 5 + t // 2, (t % 2) * S:(t % 2) * S + S],
                                                  mod_s[:, bass.ds(q * QT + t, 1)], mod_b[:, bass.ds(q * QT + t, 1)],
                                                  ALU.mult, ALU.add)
                ins.then_inc(h_ready, 1)
                dve.wait_ge(h_hi, n + 1)
                dve.wait_ge(h_ready, n + 1)
                nc.vector.tensor_tensor(op_lo[:, tile:tile + QT, :], h32[:, :, :],
                                        op_hi[:, tile:tile + QT, :].bitcast(F32), ALU.subtract).then_inc(h_lo, 1)

            for j in range(8):
                add_ada(ADA0, j, 0, ada_acc[:, j // 4, :], j % 4)
            mod_columns(0, C_GM, 0)
            modulate(0, 0, 0)

            def add_window(q, v, w):
                dve.wait_ge(w_used, used(IN, v + 1))
                b = 2 * (w % 2)
                dst = proj[:, WIN_TILE[w]:WIN_TILE[w] + CT, :]
                nc.vector.tensor_tensor(dst, dst, ps[:, b:b + 2, :].rearrange("p a (t n) -> p (a t) n", t=2),
                                        ALU.add).then_inc(win_added, 1)

            def in_phase(seg, i, q):
                for w in range(NWIN):
                    add_ada(seg, 2 * w, i, ada_acc[:, w // 4, :], w % 4)
                    split_lo(seg, 2 * w + 1, i)
                    if w == 1:
                        dve.wait_ge(ki_hi_done, q + 1)
                        nc.vector.tensor_tensor(ki_lo[:, :, :], ki_raw[:, :, :], ki_hi[:, :, :].bitcast(F32),
                                                ALU.subtract).then_inc(ki_split, 1)
                    if w >= 2:
                        add_window(q, q * NWIN + w - 2, w - 2)
                    if w == 5:
                        dve.wait_ge(ki_used, q + 1)
                        nc.vector.tensor_tensor(proj[0:SMALL, T_KI, :], proj[0:SMALL, T_KI, :],
                                                ps[0:SMALL, 4, 0:S], ALU.add).then_inc(ki_added, 1)
                if seg is IN:
                    mod_columns(q + 1, C_GM, q + 1)
                add_window(q, q * NWIN + 6, 6)
                add_window(q, q * NWIN + 7, 7)
                if seg is IN:
                    modulate(q + 1, q + 1, 0)

            dve.wait_ge(proj_zero, 1)
            nc.vector.memset(stat[:, 0:1], 0.0).then_inc(win_added, 1)
            with dve.Fori(0, 3) as q:
                in_phase(IN, q, q)
            in_phase(IN3, 0, 3)

            dve.wait_ge(masks_ready, 1)
            for n in range(NB):
                dve.wait_ge(vT_ps, 1)
                ins = nc.vector.tensor_copy(v_tok[:, n, :, :], ps[:, 4 + n, :].rearrange("p (a d) -> p a d", a=4))
            ins.then_inc(v_ready, 1)
            nc.vector.tensor_scalar(w_tok[:, :, :], ps[:, 6, 0:2 * P].rearrange("p (b n) -> p b n", b=NB),
                                    (IDXD ** -0.5) * (IDXH ** -0.5), None, ALU.mult).then_inc(v_ready, 1)
            dve.wait_ge(v_ready, 2)

            for n in range(8):
                blk, hh = divmod(n, 4)
                w = P * (blk + 1)
                dve.wait_ge(idx_relu, n + 1)
                for r in range(4):
                    head = 4 * hh + (0, 2, 1, 3)[r]
                    wcol = w_tok[:, blk, IDXD + head:IDXD + head + 1]
                    if hh == 0 and r == 0:
                        ins = nc.vector.tensor_scalar(score[:, blk, 0:w], logit[:, n % 2, r, 0:w], wcol, None,
                                                      ALU.mult)
                    else:
                        ins = nc.vector.scalar_tensor_tensor(score[:, blk, 0:w], logit[:, n % 2, r, 0:w], wcol,
                                                             score[:, blk, 0:w], ALU.mult, ALU.add)
                    ins.then_inc(idx_sum, 1)
                    dve.wait_ge(idx_sum, 4 * n + r + 1)
                if n % 4 == 0:
                    dve.wait_ge(gate_ps, n // 4 + 1)
                add_ada(MID, n, 0, ada_acc[:, n // 4, :], n % 4)

            dve.wait_ge(masks_ready, 6)
            for blk in range(NB):
                w = P * (blk + 1)
                m = slice(blk * P, blk * P + w)
                link(nc.vector.tensor_tensor(score[:, blk, 0:w], score[:, blk, 0:w], mask_c[:, m], ALU.add))
                for _ in range(TOPK // 8):
                    link(nc.vector.max(top8[:, :], score[:, blk, 0:w]))
                    link(nc.vector.match_replace(score[:, blk, 0:w], top8[:, :], score[:, blk, 0:w], TAKEN))
                link(nc.vector.tensor_scalar(mask_a[:, m], score[:, blk, 0:w], TAKEN / 2, NEG, ALU.is_gt, ALU.mult))
                link(nc.vector.tensor_tensor(mask_a[:, m], mask_a[:, m], mask_c[:, m], ALU.min))

            dve.wait_ge(sink_in, 16)

            def front(u):
                g, b = divmod(u, NB)
                w = P * (b + 1)
                m = slice(b * P, b * P + w)
                mask = mask_w if g < KV else mask_a
                dve.wait_ge(lg_ps, u + 1)
                if u >= 2:
                    dve.wait_ge(pT_ps, u - 1)
                for r in range(4):
                    slope = SLOPE[2 * (4 * (g % KV) + r) + (1 if g < KV else 0)]
                    link(nc.vector.scalar_tensor_tensor(bias[:, r % 2, 0:w], dist[:, m], -slope, mask[:, m],
                                                        ALU.mult, ALU.add))
                    head = 4 * (g % KV) + r
                    least = sink_row[:, head:head + 1] if g < KV else -3e38
                    ins = nc.vector.tensor_tensor_reduce(logit[:, u % 2, r, 0:w],
                                                   ps[:, 2 * (u % 2) + r // 2, (r % 2) * S:(r % 2) * S + w],
                                                   bias[:, r % 2, 0:w], 1.0, least, ALU.add, ALU.max,
                                                   mx[:, u % 2, r:r + 1])
                link(ins)
                ins = nc.vector.tensor_scalar(nmx[:, u % 2, :], mx[:, u % 2, :], -1.0, None, ALU.mult)
                if g < KV:
                    ins = nc.vector.tensor_tensor(sink_d[:, u % 2, :], sink_row[:, 4 * g:4 * g + 4],
                                                  mx[:, u % 2, :], ALU.subtract)
                ins.then_inc(lg_done, 1)

            def back(u):
                g, b = divmod(u, NB)
                w = P * (b + 1)
                dve.wait_ge(e_done, u + 1)
                if g < KV:
                    link(nc.vector.tensor_tensor(den[:, u % 2, :], den[:, u % 2, :], sink_e[:, u % 2, :], ALU.add))
                link(nc.vector.reciprocal(rden[:, u % 2, :], den[:, u % 2, :]))
                for r in range(4):
                    ins = nc.vector.tensor_scalar(logit[:, u % 2, r, 0:w], logit[:, u % 2, r, 0:w],
                                                  rden[:, u % 2, r:r + 1], None, ALU.mult)
                ins.then_inc(p_ready, 1)

            def tail(u):
                g, b = divmod(u, NB)
                t = (HEADS if g < KV else 0) + 4 * (g % KV)
                dve.wait_ge(o_hi, u + 1)
                nc.vector.tensor_tensor(op_lo[:, t:t + 4, b * P:(b + 1) * P],
                                        ps[:, 6, :].rearrange("p (h q) -> p h q", h=4),
                                        op_hi[:, t:t + 4, b * P:(b + 1) * P].bitcast(F32), ALU.subtract)\
                    .then_inc(o_lo, 1)

            front(0)
            for u in range(8):
                if u < 7:
                    front(u + 1)
                back(u)
                if u:
                    tail(u - 1)
            tail(7)

            def add_mix(h):
                dve.wait_ge(w_used, used(MID, MID.of_kind("W", MID.js("W")[8 * h + 7])))
                if h == 0:
                    dve.wait_ge(gate_done, NQ)
                for b in range(NB):
                    bank = 4 * h + 2 * b
                    step = 4 * h + 2 * b
                    mixed = ps[:, bank:bank + 2, :].rearrange("p a n -> p (a n)")
                    tmp = h32[:, :, :].rearrange("p a n -> p (a n)")
                    nc.vector.tensor_tensor(tmp, mixed, gate_row[:, h * 1024:(h + 1) * 1024], ALU.mult)\
                        .then_inc(mix_step, 1)
                    dve.wait_ge(mix_step, step + 1)
                    dst = x_sb[:, b, h * 1024:(h + 1) * 1024]
                    nc.vector.tensor_tensor(dst, dst, tmp, ALU.add).then_inc(mix_step, 1)
                    dve.wait_ge(mix_step, step + 2)

            for n, j in enumerate(MID.js("W")):
                split_lo(MID, j)
                if n == 9:
                    dve.wait_ge(mod2_ps, 1)
                    nc.vector.scalar_tensor_tensor(mod_s[:, :], ps[:, 7, 0:KT], 1.0, cols[:, C_GF, 0:KT],
                                                   ALU.add, ALU.mult).then_inc(mod2_done, 1)
                    nc.vector.tensor_copy(mod_b[:, :], ps[:, 7, KT:2 * KT]).then_inc(mod2_done, 1)
                    dve.wait_ge(mod2_done, 2)
                if n == 11:
                    add_mix(0)
            add_mix(1)
            rms(1)
            modulate(0, NQ, 0)
            for q in range(NQ):
                split_lo(UP0, 2 * q)
                split_lo(UP0, 2 * q + 1)
                if q < NQ - 1:
                    modulate(q + 1, NQ + q + 1, QT * (q + 1))

            def conv_taps(g):
                for n, t in enumerate(TILE_ORDER):
                    dve.wait_ge(conv_a, g * CT + n + 1)
                    for lag, tap in ((1, C_W1), (2, C_W0)):
                        gate_ps_t = ps[:, t // 2, (t % 2) * S:(t % 2) * S + S - lag]
                        ins = nc.vector.scalar_tensor_tensor(conv[:, t, lag:S], gate_ps_t,
                                                             cols[:, tap, bass.ds(g * CT + t, 1)],
                                                             conv[:, t, lag:S], ALU.mult, ALU.add)
                        ins.then_inc(conv_step, 1)
                        dve.wait_ge(conv_step, g * 2 * CT + 2 * n + lag)
                dve.wait_ge(silu_done, g + 1)
                nc.vector.tensor_tensor(conv[:, :, :], conv[:, :, :],
                                        ps[:, 2:4, :].rearrange("p a (t n) -> p (a t) n", t=2), ALU.mult)\
                    .then_inc(gu_done, 1)
                dve.wait_ge(act_hi_done, g + 1)
                dve.wait_ge(gu_done, g + 1)
                nc.vector.tensor_tensor(act_lo[:, :, :], conv[:, :, :], act_hi[:, :, :].bitcast(F32),
                                        ALU.subtract).then_inc(act_split, 1)

            def add_y(h, count):
                dve.wait_ge(w_used, count)
                dst = y[:, :, h * 1024:(h + 1) * 1024]
                nc.vector.tensor_tensor(dst, dst, ps[:, 4:8, :].rearrange("p (b a) n -> p b (a n)", b=NB),
                                        ALU.add).then_inc(y_added, 1)

            def ffn_body(seg, i, g):
                a = 0
                w_js = seg.js("W")
                w = 0
                for j, kind in enumerate(seg.kinds):
                    if kind == "A":
                        add_ada(seg, j, i, gate_row[:, bass.ds(i * CW, CW)], a)
                        a += 1
                        continue
                    split_lo(seg, j, i)
                    if w == 1:
                        conv_taps(g - 1)
                    if w == 3:
                        add_y(1, used(seg, seg.of_kind("W", w_js[0], i) - 1))
                    if w == 8:
                        add_y(0, used(seg, seg.of_kind("W", w_js[5], i)))
                    w += 1

            link(nc.vector.memset(ps[:, 4:8, :], 0.0))
            dve.wait_ge(y_zero, 1)
            with dve.Fori(0, FFN_A.times) as i:
                ffn_body(FFN_A, i, i + 1)
            with dve.Fori(0, FFN.times) as i:
                ffn_body(FFN, i, i + 1 + FFN_A.times)
            split_lo(LAST, 0)
            split_lo(LAST, 1)
            conv_taps(PASSES - 1)
            add_y(1, used(LAST, LAST.of_kind("W", 0) - 1))
            split_lo(LAST, 2)
            split_lo(LAST, 3)
            add_y(0, used(LAST, LAST.of_kind("W", 1)))
            add_y(1, used(LAST, LAST.of_kind("W", 3)))
            dve.wait_ge(gate2_ps, 1)
            dve.wait_ge(y_added, 2 * PASSES + 1)
            for b in range(NB):
                yb = y[:, b, :]
                nc.vector.tensor_tensor(yb, yb, ps[:, 0:4, :].rearrange("p a n -> p (a n)"), ALU.mult)\
                    .then_inc(x_step, 1)
                dve.wait_ge(x_step, 2 * b + 1)
                nc.vector.tensor_tensor(x_sb[:, b, :], x_sb[:, b, :], yb, ALU.add).then_inc(x_step, 1)
            rms(2)
            dve.wait_ge(rstd_done, 3)
            dve.wait_ge(gf_in, 16)
            for b in range(NB):
                nc.vector.scalar_tensor_tensor(raw[:, 2 + b, :], x_sb[:, b, :], stat[:, 6 + b:7 + b],
                                               raw[:, 0, :], ALU.mult, ALU.mult).then_inc(y_ready, 1)

        @block.tensor
        def _(pe):
            def three(dst, s_hi, s_lo, m_hi, m_lo, first, last, more=True):
                nc.tensor.matmul(dst, s_hi, m_hi, start=first, stop=False, skip_group_check=True)
                nc.tensor.matmul(dst, s_hi, m_lo, start=False, stop=False, skip_group_check=True)
                return nc.tensor.matmul(dst, s_lo, m_hi, start=False, stop=last, skip_group_check=True)

            pe.wait_ge(const_ready, 4)
            pe.wait_ge(c_act, 1)
            pe.wait_ge(rows_in, 16 * 7)
            pe.wait_ge(sq_done, 2)
            nc.tensor.transpose(ps[:, 7, 0:KT], rows[0:KT, C_C, :], ident[0:KT, 0:KT]).then_inc(cols_ps, 1)
            for n in range(6):
                mm = nc.tensor.transpose(ps[:, 6, n * 44:(n + 1) * 44], rows[0:44, 1 + n, :], ident[0:44, 0:44])
            mm.then_inc(cols_ps, 1)
            pe.wait_ge(cols_ready, 2)
            pe.sem_inc(w_used, PAIR)

            def turn_xn(n):
                pe.wait_ge(xn_ready, n + 1)
                if later(n):
                    pe.wait_ge(h_ready, n)
                for t in range(QT):
                    for b in range(NB):
                        mm = nc.tensor.transpose(ps[:, 5 + t // 2, (t % 2) * S + b * P:(t % 2) * S + (b + 1) * P],
                                                 xn[:, b, t * P:(t + 1) * P], ident[:, :])
                mm.then_inc(xnT_ready, 1)

            def reduce_mod(half, vec, q):
                for t in range(QT):
                    dst = ps[:, 7, half * QT + t:half * QT + t + 1]
                    nc.tensor.matmul(dst, ada_acc[:, half, t * P:(t + 1) * P], ones[:, 0:1],
                                     start=(half == 0 and t == 0), stop=False, skip_group_check=True)
                    mm = nc.tensor.matmul(dst, b_rows[:, t * P:(t + 1) * P],
                                          ident[0:24, bass.ds(vec * NQ + q, 1)],
                                          start=False, stop=True, skip_group_check=True)
                return mm

            def reduce_mods(chunks, q, n):
                pe.wait_ge(ada_sum, QT * chunks)
                if later(n):
                    pe.wait_ge(mod_done, 2 * n)
                reduce_mod(0, SCALE1, q)
                reduce_mod(1, SHIFT1, q).then_inc(mod_ps, 1)

            turn_xn(0)
            reduce_mods(8, 0, 0)

            def in_window(seg, i, q, w):
                j = 2 * w + 1
                pe.wait_ge(win_added, q * NWIN + w)
                pe.wait_ge(w_split, split(seg.of_kind("W", j, i)))
                hi, lo = pair_hi[seg.pair(j)], pair_lo[seg.pair(j)]
                for k in range(QT):
                    for t in range(CT):
                        s = slice(k * CW + t * P, k * CW + (t + 1) * P)
                        mm = three(ps[:, 2 * (w % 2) + t // 2, (t % 2) * S:(t % 2) * S + S],
                                   hi[:, s], lo[:, s], op_hi[:, k, :], op_lo[:, k, :],
                                   k == 0 and t % 2 == 0, k == QT - 1)
                mm.then_inc(w_used, 1)

            def in_small(q):
                pe.wait_ge(ki_split, q + 1)
                for k in range(QT):
                    mm = three(ps[0:SMALL, 4, 0:S], ki_hi[:, k, :], ki_lo[:, k, :], op_hi[:, k, :], op_lo[:, k, :],
                               k == 0, k == QT - 1)
                mm.then_inc(ki_used, 1)

            def in_phase(seg, i, q):
                pe.wait_ge(h_lo, q + 1)
                for w in range(NWIN):
                    in_window(seg, i, q, w)
                    if w == 2:
                        in_small(q)
                    if w == 3 and seg is IN:
                        turn_xn(q + 1)
                if seg is IN:
                    reduce_mods(8 * (q + 2), q + 1, q + 1)

            with pe.Fori(0, 3) as q:
                in_phase(IN, q, q)
            in_phase(IN3, 0, 3)

            def gate_bcast(n, a_count):
                pe.wait_ge(ada_sum, QT * a_count)
                if n:
                    pe.wait_ge(gate_done, n)
                else:
                    pe.wait_ge(mod_done, 2 * NQ)
                nc.tensor.matmul(ps[:, 7, :], ones[:, :], ada_acc[:, n % 2, :], start=True, stop=False)
                nc.tensor.matmul(ps[:, 7, :], ident[0:24, GATE1 * NQ + n:GATE1 * NQ + n + 1].to_broadcast([24, P]),
                                 b_rows[:, :], start=False, stop=True).then_inc(gate_ps, 1)

            base_a = IN3.of_kind("A", 15)
            gate_bcast(0, base_a)

            pe.wait_ge(win_added, NQ * NWIN + 1)
            pe.wait_ge(ki_added, NQ)
            for b in range(NB):
                for n, t in enumerate((T_VB, T_VB + 1, T_VA, T_VA + 1)):
                    nc.tensor.transpose(ps[:, 4 + b, n * P:(n + 1) * P], proj[:, t, b * P:(b + 1) * P], ident[:, :])
            for b in range(NB):
                mm = nc.tensor.transpose(ps[:, 6, b * P:(b + 1) * P], proj[:, T_KI, b * P:(b + 1) * P], ident[:, :])
            mm.then_inc(vT_ps, 1)
            gate_bcast(1, base_a)

            pe.wait_ge(dup_in, 16)
            for n in range(8):
                blk, hh = divmod(n, 4)
                w = P * (blk + 1)
                if n >= 2:
                    pe.wait_ge(idx_relu, n - 1)
                for odd in range(2):
                    rows_ = slice(IDXD * odd, IDXD * odd + IDXD)
                    keys = ki_dup[rows_, 0:w] if odd else proj[rows_, T_KI, 0:w]
                    for m in range(2):
                        t = T_QI + 2 * hh + m
                        mm = nc.tensor.matmul(ps[:, 2 * (n % 2) + odd, m * S:m * S + w],
                                              proj[rows_, t, blk * P:(blk + 1) * P], keys, start=True, stop=True)
                mm.then_inc(idx_ps, 1)
                if n == 3:
                    gate_bcast(2, base_a + 4)
                if n == 7:
                    gate_bcast(3, base_a + 8)

            mod2_js = MID.js("P")

            def mod2(n):
                j = mod2_js[n]
                col = n // 4 * CT
                k = n % 4
                pe.wait_ge(raw_in[MID.slot(j)], 16 * MID.loads(j))
                if n == 0:
                    pe.wait_ge(gate_done, NQ)
                for t in range(QT):
                    for m in range(CT):
                        mm = nc.tensor.matmul(ps[:, 7, col + m:col + m + 1],
                                              raw[:, MID.slot(j), t * CW + m * P:t * CW + (m + 1) * P],
                                              silu_c[:, k * QT + t:k * QT + t + 1],
                                              start=(n == 0 and t == 0 and m == 0), stop=False,
                                              skip_group_check=True)
                mm.then_inc(p_used, 1)

            def logits(u):
                g, b = divmod(u, NB)
                w = P * (b + 1)
                if u >= 2:
                    pe.wait_ge(lg_done, u - 1)
                elif u == 0:
                    pe.wait_ge(idx_relu, 8)
                    pe.wait_ge(q_scaled, 2)
                q0, k0 = (T_QB, T_KB) if g < KV else (T_QA, T_KA)
                for r in range(4):
                    mm = nc.tensor.matmul(ps[:, 2 * (u % 2) + r // 2, (r % 2) * S:(r % 2) * S + w],
                                          proj[:, q0 + 4 * (g % KV) + r, b * P:(b + 1) * P],
                                          proj[:, k0 + g % KV, 0:w], start=True, stop=True)
                mm.then_inc(lg_ps, 1)

            def values(u):
                g, b = divmod(u, NB)
                pe.wait_ge(p_ready, u + 1)
                pe.wait_ge(v_ready, 2)
                if u:
                    pe.wait_ge(pT_ready, u)
                for kt in range(b + 1):
                    for r in range(4):
                        mm = nc.tensor.transpose(ps[:, 4 + kt, r * P:(r + 1) * P],
                                                 logit[:, u % 2, r, kt * P:(kt + 1) * P], ident[:, :])
                mm.then_inc(pT_ps, 1)
                pe.wait_ge(pT_ready, u + 1)
                if u:
                    pe.wait_ge(o_lo, u)
                for kt in range(b + 1):
                    mm = nc.tensor.matmul(ps[:, 6, :], v_tok[:, kt, g, :], probT[:, kt, :],
                                          start=(kt == 0), stop=(kt == b))
                mm.then_inc(o_ps, 1)

            logits(0)
            logits(1)
            for u in range(8):
                values(u)
                if u < 6:
                    logits(u + 2)
                mod2(2 * u)
                mod2(2 * u + 1)

            pe.wait_ge(o_lo, 8)

            def down_chunk(seg, j, i, s_hi, s_lo, tile, bank, first, last):
                pe.wait_ge(w_split, split(seg.of_kind("W", j, i)))
                hi, lo = pair_hi[seg.pair(j)], pair_lo[seg.pair(j)]
                for k in range(2):
                    for b in range(NB):
                        tok = slice(b * P, (b + 1) * P)
                        for n, (st, w) in enumerate(((s_hi, hi), (s_hi, lo), (s_lo, hi))):
                            for a in range(2):
                                mm = nc.tensor.matmul(ps[:, bank + 2 * b + a, :], st[:, tile + k, tok],
                                                      w[:, k * 1024 + a * CW:k * 1024 + (a + 1) * CW],
                                                      start=(first and k == 0 and n == 0),
                                                      stop=(last and k == 1 and n == 2), skip_group_check=True)
                mm.then_inc(w_used, 1)

            for n, j in enumerate(MID.js("W")):
                h, pr = divmod(n, 8)
                if n == 8:
                    pe.wait_ge(mod2_done, 2)
                down_chunk(MID, j, 0, op_hi, op_lo, 2 * pr, 4 * h, pr == 0, pr == 7)
                if h == 0:
                    mod2(16 + 2 * n)
                    mod2(17 + 2 * n)
                if n == 7:
                    for half, vec in ((0, SCALE2), (1, SHIFT2)):
                        for t in range(QT):
                            mm = nc.tensor.matmul(ps[:, 7, half * KT + t:half * KT + KT:QT],
                                                  b_rows[:, t * P:(t + 1) * P],
                                                  ident[0:24, vec * NQ:vec * NQ + NQ],
                                                  start=False, stop=True, skip_group_check=True)
                    mm.then_inc(mod2_ps, 1)

            def up_chunk(seg, j, i, n, inc=1):
                pe.wait_ge(w_split, split(seg.of_kind("W", j, i)))
                hi, lo = pair_hi[seg.pair(j)], pair_lo[seg.pair(j)]
                q = n // 2
                for k in range(QT):
                    for t in range(CT):
                        cs = slice(k * CW + t * P, k * CW + (t + 1) * P)
                        mm = three(ps[:, 2 * (n % 2) + t // 2, (t % 2) * S:(t % 2) * S + S],
                                   hi[:, cs], lo[:, cs], op_hi[:, q * QT + k, :], op_lo[:, q * QT + k, :],
                                   q == 0 and k == 0 and t % 2 == 0, q == NQ - 1 and k == QT - 1)
                mm.then_inc(w_used, inc)

            turn_xn(NQ)
            turn_xn(NQ + 1)
            for n in range(8):
                if n in (1, 3):
                    turn_xn(NQ + 2 + n // 2)
                pe.wait_ge(h_lo, NQ + n // 2 + 1)
                up_chunk(UP0, n, 0, n, 3 if n == 7 else 1)

            def ffn_body(seg, i, g):
                js = seg.js("W")
                pe.wait_ge(gu_done, g)
                for n in range(4):
                    up_chunk(seg, js[n], i, n)
                pe.wait_ge(act_split, g)
                pe.wait_ge(y_added, 2 * g - 1)
                for n in range(2):
                    down_chunk(seg, js[4 + n], i, act_hi, act_lo, 2 * n, 4, n == 0, n == 1)
                for n in range(4, 8):
                    up_chunk(seg, js[2 + n], i, n)
                pe.wait_ge(y_added, 2 * g)
                for n in range(2):
                    down_chunk(seg, js[10 + n], i, act_hi, act_lo, 2 * n, 4, n == 0, n == 1)

            with pe.Fori(0, FFN_A.times) as i:
                ffn_body(FFN_A, i, i + 1)
            with pe.Fori(0, FFN.times) as i:
                ffn_body(FFN, i, i + 1 + FFN_A.times)
            pe.wait_ge(act_split, PASSES)
            pe.wait_ge(y_added, 2 * PASSES - 1)
            for n in range(2):
                down_chunk(LAST, n, 0, act_hi, act_lo, 2 * n, 4, n == 0, n == 1)
            pe.wait_ge(ada_sum, QT * FFN.before["A"])
            for n in range(NQ):
                nc.tensor.matmul(ps[:, n, :], ones[:, :], gate_row[:, n * CW:(n + 1) * CW], start=True, stop=False)
                mm = nc.tensor.matmul(ps[:, n, :],
                                      ident[0:24, GATE2 * NQ + n:GATE2 * NQ + n + 1].to_broadcast([24, P]),
                                      b_rows[:, :], start=False, stop=True)
            mm.then_inc(gate2_ps, 1)
            pe.wait_ge(y_added, 2 * PASSES)
            for n in range(2):
                down_chunk(LAST, 2 + n, 0, act_hi, act_lo, 2 * n, 4, n == 0, n == 1)


_INS = ['x', 'c', 'w_ada', 'b_ada', 'g_mix', 'w_in', 'sinks', 'w_o', 'g_ffn', 'w_gate', 'w_up', 'conv_w',
        'conv_b', 'w_down', 'g_final']
_OUTS = [((1, S, D), 'float32')]


def kernel(**inputs):
    import numpy as _np
    import concourse.bacc as _bacc
    from concourse import mybir as _mybir
    from concourse.bass_utils import run_bass_kernel_spmd as _run

    nc = _bacc.Bacc("TRN2", target_bir_lowering=False, num_devices=1)
    arrays, args = {}, []
    for name in _INS:
        a = _np.ascontiguousarray(inputs[name])
        arrays[f"in_{name}_dram"] = a
        args.append(nc.dram_tensor(f"in_{name}_dram", a.shape, _mybir.dt.from_np(a.dtype), kind="ExternalInput").ap())
    for i, (shape, dtype) in enumerate(_OUTS):
        dt = _mybir.dt.from_np(_np.dtype(dtype))
        args.append(nc.dram_tensor(f"out_{i}_dram", shape, dt, kind="ExternalOutput").ap())
    program(nc, *args)
    r = _run(nc, [arrays], core_ids=[0])
    got = tuple(r.results[0][f"out_{i}_dram"] for i in range(len(_OUTS)))
    return got[0]
```

```python
from contextlib import ExitStack

import concourse.bass as bass
from concourse import mybir

ALU = mybir.AluOpType
ACT = mybir.ActivationFunctionType
AX = mybir.AxisListType
F32 = mybir.dt.float32
F32R = mybir.dt.float32r

P = 128
D = 2048
S = 256
HD = 128
KT = D // P
NB = S // P
HEADS = 8
KV = 2
IDXH = 16
IDXD = 64
TOPK = min(256, S // 4)
WINDOW = 128
F = 11 * D // 4
FT = F // P
EPS = 1e-6
NEG = -1e30
TAKEN = -3e38
NQ = 4
QT = KT // NQ
CW = 512
CT = CW // P
RAW = 4
PAIR = 4
PASSES = F // CW
SMALL = IDXD + IDXH
IN_W = 2 * (HEADS + 2 * KV) * HD + IDXH * IDXD + SMALL
T_QA, T_KA, T_VA, T_QI, T_KI, T_QB, T_KB, T_VB = 0, 8, 10, 12, 20, 21, 29, 31
NT = 33
TILE_ORDER = [0, 2, 1, 3]
WIN_COL = [0, 512, 1024, 1536, 2048, 2640, 3152, 3664]
WIN_TILE = [0, 4, 8, 12, 16, 21, 25, 29]
SMALL_COL = 2560
NWIN = len(WIN_COL)
SLOPE = [2.0 ** (-8.0 * (n + 1) / (2 * HEADS)) for n in range(2 * HEADS)]
SHIFT1, SCALE1, GATE1, SHIFT2, SCALE2, GATE2 = range(6)

SEG_ADA0 = ("A" * 8, 1)
SEG_IN = ("A" + "AW" * 7 + "W", 3)
SEG_IN3 = ("A" + "AW" * 7 + "W", 1)
SEG_MID = ("QA" * 4 + "Q" * 12 + "AAW" * 6 + "AW" * 8 + "WW", 1)
SEG_UP0 = ("W" * 8, 1)
SEG_FFN_A = ("WWWAWWWAWWWAWWWA", 4)
SEG_FFN = ("W" * 12, 6)
SEG_LAST = ("W" * 4, 1)
SEGS = [SEG_ADA0, SEG_IN, SEG_IN3, SEG_MID, SEG_UP0, SEG_FFN_A, SEG_FFN, SEG_LAST]


def later(n):
    return not (isinstance(n, int) and n == 0)


GATE_BANK = [5, 6, 5, 6]


class Stream:

    def __init__(self, index):
        self.kinds, self.times = SEGS[index]
        self.before = {k: sum(s.count(k) * t for s, t in SEGS[:index]) for k in "AWQ"}
        self.start = sum(len(s) * t for s, t in SEGS[:index])

    def number(self, j, i=0):
        return self.start + i * len(self.kinds) + j

    def slot(self, j):
        return (self.start + j) % RAW

    def loads(self, j, i=0):
        return (self.start + j) // RAW + 1 + i * (len(self.kinds) // RAW)

    def of_kind(self, k, j, i=0):
        return self.before[k] + i * self.kinds.count(k) + self.kinds[:j + 1].count(k)

    def pair(self, j):
        return (self.of_kind("W", j) - 1) % PAIR

    def js(self, k):
        return [j for j, x in enumerate(self.kinds) if x == k]


ADA0, IN, IN3, MID, UP0, FFN_A, FFN, LAST = (Stream(n) for n in range(len(SEGS)))


def program(nc, x, c, w_ada, b_ada, g_mix, w_in, sinks, w_o, g_ffn, w_gate, w_up, conv_w, conv_b,
            w_down, g_final, out):
    ctx = ExitStack()
    with ctx:
        def sb(name, shape, dt=F32):
            return ctx.enter_context(nc.sbuf_tensor(name, shape, dt))

        def sem(name):
            return ctx.enter_context(nc.semaphore(name))

        x_sb = sb("x_sb", [P, NB, D])
        op_hi = sb("op_hi", [P, KT, S], F32R)
        op_lo = sb("op_lo", [P, KT, S], F32R)
        raw = sb("raw", [P, RAW, 2048])
        pair_hi = [None] * PAIR
        pair_lo = [None] * PAIR
        for n in range(2):
            pair_hi[n] = sb(f"pair_hi{n}", [P, 2048], F32R)
            pair_lo[n] = sb(f"pair_lo{n}", [P, 2048], F32R)
        h32 = sb("h32", [P, QT, S])
        xn = sb("xn", [P, NB, CW])
        ada_acc = sb("ada_acc", [P, 2, CW])
        with nc.sbuf_tensor("rows", [44, 6, P], F32) as rows:
            pass
        gate_row = sb("gate_row", [P, D])
        ki_raw = sb("ki_raw", [P, QT, SMALL])
        ki_hi = sb("ki_hi", [P, QT, SMALL], F32R)
        ki_lo = sb("ki_lo", [P, QT, SMALL], F32R)
        ident = sb("ident", [P, P])
        ones = sb("ones", [P, P])
        b_rows = sb("b_rows", [24, CW])
        cols = sb("cols", [P, 6, 44])
        silu_c = sb("silu_c", [P, KT])
        c_rows = sb("c_rows", [KT, P])
        b_cols = sb("b_cols", [P, QT, 24])
        mod_s = sb("mod_s", [P, KT])
        mod_b = sb("mod_b", [P, KT])
        sink_row = sb("sink_row", [P, HEADS])
        stat = sb("stat", [P, 10])

        with ExitStack() as att:
            def sba(name, shape, dt=F32):
                return att.enter_context(nc.sbuf_tensor(name, shape, dt))
            logit = sba("logit", [P, 2, 4, S])
            probT = sba("probT", [P, 2, 4 * P])
            v_tok = sba("v_tok", [P, NB, 4, HD])
            score = sba("score", [P, NB, S])
            w_tok = sba("w_tok", [P, NB, P])
            bias = sba("bias", [P, 2, S])
            dist = sba("dist", [P, 3 * P])
            mask_c = sba("mask_c", [P, 3 * P])
            mask_w = sba("mask_w", [P, 3 * P])
            mask_a = sba("mask_a", [P, 3 * P])
            top8 = sba("top8", [P, 8])
            mx = sba("mx", [P, 2, 4])
            nmx = sba("nmx", [P, 2, 4])
            den = sba("den", [P, 2, 4])
            sink_e = sba("sink_e", [P, 2, 4])
            sink_d = sba("sink_d", [P, 2, 4])
            rden = sba("rden", [P, 2, 4])
            ki_dup = sba("ki_dup", [P, S])
        for n in range(2, PAIR):
            pair_hi[n] = sb(f"pair_hi{n}", [P, 2048], F32R)
            pair_lo[n] = sb(f"pair_lo{n}", [P, 2048], F32R)
        with ExitStack() as ffn:
            def sbf(name, shape, dt=F32):
                return ffn.enter_context(nc.sbuf_tensor(name, shape, dt))
            act_hi = sbf("act_hi", [P, CT, S], F32R)
            act_lo = sbf("act_lo", [P, CT, S], F32R)
            conv = sbf("conv", [P, CT, S])
            y = sbf("y", [P, NB, D])
        proj = sb("proj", [P, NT, S])

        ps = ctx.enter_context(nc.psum_tensor("ps", [P, 8, 512], F32))

        raw_in = [sem(f"raw_in{n}") for n in range(RAW)]
        pair_in = [sem(f"pair_in{n}") for n in range(RAW)]
        ada_sum = sem("ada_sum")
        w_split = sem("w_split")
        q_used = sem("q_used")
        w_hi = sem("w_hi")
        w_used = sem("w_used")
        x_in = [sem(f"x_in{b}") for b in range(NB)]
        c_in = sem("c_in")
        rows_in = sem("rows_in")
        sink_in = sem("sink_in")
        const_ready = sem("const_ready")
        masks_ready = sem("masks_ready")
        c_act = sem("c_act")
        cols_ps = sem("cols_ps")
        cols_ready = sem("cols_ready")
        sq_done = sem("sq_done")
        var_done = sem("var_done")
        root_done = sem("root_done")
        rstd_done = sem("rstd_done")
        xn_ready = sem("xn_ready")
        xnT_ready = sem("xnT_ready")
        mod_ps = sem("mod_ps")
        mod_done = sem("mod_done")
        h_ready = sem("h_ready")
        h_hi = sem("h_hi")
        h_lo = sem("h_lo")
        ki_in = sem("ki_in")
        ki_hi_done = sem("ki_hi_done")
        ki_split = sem("ki_split")
        ki_used = sem("ki_used")
        win_added = sem("win_added")
        ki_added = sem("ki_added")
        proj_zero = sem("proj_zero")
        bank_zero = sem("bank_zero")
        gate_ps = sem("gate_ps")
        gate_done = sem("gate_done")
        q_scaled = sem("q_scaled")
        dup_in = sem("dup_in")
        vT_ps = sem("vT_ps")
        v_ready = sem("v_ready")
        idx_ps = sem("idx_ps")
        idx_relu = sem("idx_relu")
        idx_sum = sem("idx_sum")
        lg_ps = sem("lg_ps")
        lg_done = sem("lg_done")
        e_done = sem("e_done")
        p_ready = sem("p_ready")
        pT_ps = sem("pT_ps")
        pT_ready = sem("pT_ready")
        o_ps = sem("o_ps")
        o_hi = sem("o_hi")
        o_lo = sem("o_lo")
        mix_step = sem("mix_step")
        rows2_ps = sem("rows2_ps")
        rows2_done = sem("rows2_done")
        mod2_ps = sem("mod2_ps")
        mod2_done = sem("mod2_done")
        gate_zero = sem("gate_zero")
        y_zero = sem("y_zero")
        conv_a = sem("conv_a")
        conv_step = sem("conv_step")
        silu_done = sem("silu_done")
        gu_done = sem("gu_done")
        act_hi_done = sem("act_hi_done")
        act_split = sem("act_split")
        y_added = sem("y_added")
        gate2_ps = sem("gate2_ps")
        x_step = sem("x_step")
        gf_in = sem("gf_in")
        y_ready = sem("y_ready")
        out_done = sem("out_done")
        chain = sem("chain")

        C_GM, C_GF, C_W0, C_W1, C_W2, C_B = range(6)

        def in_chunk(q, w):
            return w_in[0, bass.ds(q * CW, CW), WIN_COL[w]:WIN_COL[w] + CW]

        def quarter(ap):
            return ap.rearrange("(k p) n -> p k n", p=P)

        def used(seg, count):
            return PAIR + count + (2 if seg in (FFN_A, FFN, LAST) else 0)

        UP_END = PAIR + UP0.of_kind("W", 7)

        def split(count):
            return count + RAW

        def sums(count, seg=None):
            if seg is IN or seg is None and count <= PAIRED:
                return 2 * count
            return PAIRED + count

        PAIRED = IN3.before["A"]

        block = ctx.enter_context(nc.Block())

        @block.sync
        def _(sp):
            segs = [ADA0, IN, IN3, MID, UP0, FFN_A, FFN, LAST]

            def load(seg, j, i, src, tiles=QT):
                waits = []
                if seg is not ADA0 or j >= RAW:
                    if j >= RAW:
                        need = {seg.kinds[j - RAW]: seg.of_kind(seg.kinds[j - RAW], j - RAW, i)}
                    else:
                        ends = [segs[segs.index(seg) - 1].kinds] + [seg.kinds] * (seg.times > 1)
                        need = {}
                        for kind in {end[j - RAW] for end in ends}:
                            after = min(end[len(end) + j - RAW + 1:].count(kind)
                                        for end in ends if end[j - RAW] == kind)
                            need[kind] = seg.before[kind] - after + i * seg.kinds.count(kind)
                    for kind, count in need.items():
                        what, count = {"A": (ada_sum, sums(count, seg if seg.times > 1 else None)),
                                       "W": (w_split, split(count)), "Q": (q_used, count)}[kind]
                        waits.append((what, sp.lower_val(count)))
                if len(waits) == 2:
                    sp.wait_ge(*waits[1])
                dst = raw[:, seg.slot(j), :].rearrange("p (k n) -> p k n", k=tiles)
                if isinstance(src, list):
                    dst = raw[:, seg.slot(j), :].rearrange("p (k v n) -> p k v n", k=2, v=2)
                    dma = sp.dma_start(dst[:, 0], src[0])
                    dma.then_inc(raw_in[seg.slot(j)], 16)
                    sp.dma_start(dst[:, 1], src[1]).then_inc(pair_in[seg.slot(j)], 16)
                else:
                    dma = sp.dma_start(dst, src)
                    dma.then_inc(raw_in[seg.slot(j)], 16)
                if waits:
                    dma.wait_op(*waits[0], "sem-ge")

            def ada_pair(q, n):
                return [w_ada[0, (2 * n + k) * P:(2 * n + k + 1) * P, SHIFT1 * D:(SCALE1 + 1) * D]
                        .rearrange("p (v c) -> p v c", v=2)[:, :, bass.ds(q * CW, CW)] for k in range(2)]

            def ada(which, k):
                return w_ada[0, bass.ds(k * P, P), which * D:(which + 1) * D].rearrange("p (k n) -> p k n", k=1)

            sp.dma_start(ki_raw[:, :, :], quarter(w_in[0, 0:CW, SMALL_COL:SMALL_COL + SMALL]))\
                .then_inc(ki_in, 16)
            for j in range(8):
                load(ADA0, j, 0, ada_pair(0, j))
            in_load = {}
            with sp.Fori(0, 3) as q:
                for n, j in enumerate(IN.js("A")):
                    in_load[j] = ada_pair(q + 1, n)
                for w, j in enumerate(IN.js("W")):
                    in_load[j] = quarter(in_chunk(q, w))
                for j in range(len(IN.kinds)):
                    load(IN, j, q, in_load[j])
                sp.wait_ge(ki_split, q + 1)
                sp.wait_ge(ki_in, 16)
                sp.dma_start(ki_raw[:, :, :],
                             quarter(w_in[0, bass.ds((q + 1) * CW, CW), SMALL_COL:SMALL_COL + SMALL]))\
                    .then_inc(ki_in, 16)
            for n, j in enumerate(IN3.js("A")):
                in_load[j] = ada(GATE1, n)
            for w, j in enumerate(IN3.js("W")):
                in_load[j] = quarter(in_chunk(3, w))
            for j in range(len(IN3.kinds)):
                load(IN3, j, 0, in_load[j], 1 if IN3.kinds[j] == "A" else QT)
            mid_a = iter([ada(GATE1, n) for n in range(8, KT)] + [ada(SHIFT2, n) for n in range(KT)])
            mid_q = iter([ada(SCALE2, n) for n in range(KT)])
            mid_w = iter([w_o[0, n * 2 * P:(n + 1) * 2 * P, h * 1024:(h + 1) * 1024]
                          .rearrange("(k p) n -> p k n", p=P) for h in range(2) for n in range(8)])
            for j, kind in enumerate(MID.kinds):
                load(MID, j, 0, next({"A": mid_a, "Q": mid_q, "W": mid_w}[kind]), 2 if kind == "W" else 1)

            def up(g, n):
                w = (w_gate, w_up)[n % 2]
                return quarter(w[0, (n // 2) * CW:(n // 2 + 1) * CW, bass.ds(g * CW, CW)])

            def down(g, n):
                return w_down[0, bass.ds(g * CW + (n % 2) * 2 * P, 2 * P),
                              (n // 2) * 1024:(n // 2 + 1) * 1024].rearrange("(k p) n -> p k n", p=P)

            def ffn_body(seg, i, g):
                ws = iter([(up(g, n), QT) for n in range(4)] + [(down(g - 1, n), 2) for n in range(2)]
                          + [(up(g, n), QT) for n in range(4, 8)] + [(down(g - 1, n), 2) for n in range(2, 4)])
                a = 0
                for j, kind in enumerate(seg.kinds):
                    if kind == "A":
                        load(seg, j, i, ada(GATE2, i * QT + a), 1)
                        a += 1
                    else:
                        src, tiles = next(ws)
                        load(seg, j, i, src, tiles)

            for n in range(8):
                load(UP0, n, 0, up(0, n))
            with sp.Fori(0, FFN_A.times) as i:
                ffn_body(FFN_A, i, i + 1)
            with sp.Fori(0, FFN.times) as i:
                ffn_body(FFN, i, i + 1 + FFN_A.times)
            for n in range(4):
                load(LAST, n, 0, down(PASSES - 1, n), 2)
            sp.wait_ge(w_split, split(LAST.of_kind("W", 3)))
            sp.dma_start(raw[:, 0, :], g_final[None, :].to_broadcast([P, D])).then_inc(gf_in, 16)
            for b in range(NB):
                sp.wait_ge(y_ready, b + 1)
                sp.dma_start(out[0, b * P:(b + 1) * P, :], raw[:, 2 + b, :]).then_inc(out_done, 16)
            sp.wait_ge(out_done, 16 * NB)

        @block.gpsimd
        def _(pool):
            nc.gpsimd.memset(ident[:, :], 0.0).then_inc(const_ready, 1)
            pool.wait_ge(const_ready, 1)
            nc.gpsimd.affine_select(out=ident[:, :], in_=ident[:, :], compare_op=ALU.not_equal, fill=1.0,
                                    base=0, pattern=[[-1, P]], channel_multiplier=1).then_inc(const_ready, 1)
            nc.gpsimd.memset(rows[:, :, :], 0.0).then_inc(const_ready, 1)
            nc.gpsimd.memset(ones[:, :], 1.0).then_inc(const_ready, 1)
            nc.gpsimd.memset(proj[:, :, :], 0.0).then_inc(proj_zero, 1)
            pool.wait_ge(w_used, used(IN3, IN3.of_kind("W", 15)))
            nc.gpsimd.iota(dist[:, 0:P], pattern=[[-1, P]], base=0, channel_multiplier=1,
                           allow_small_or_imprecise_dtypes=True)
            nc.gpsimd.iota(dist[:, P:3 * P], pattern=[[-1, S]], base=P, channel_multiplier=1,
                           allow_small_or_imprecise_dtypes=True).then_inc(masks_ready, 1)
            nc.gpsimd.memset(mask_c[:, :], 0.0).then_inc(masks_ready, 1)
            pool.wait_ge(masks_ready, 2)
            nc.gpsimd.affine_select(out=mask_c[:, 0:P], in_=mask_c[:, 0:P], compare_op=ALU.is_ge, fill=NEG,
                                    base=0, pattern=[[-1, P]], channel_multiplier=1).then_inc(masks_ready, 1)
            nc.gpsimd.affine_select(out=mask_c[:, P:3 * P], in_=mask_c[:, P:3 * P], compare_op=ALU.is_ge,
                                    fill=NEG, base=P, pattern=[[-1, S]], channel_multiplier=1)\
                .then_inc(masks_ready, 1)
            pool.wait_ge(masks_ready, 4)
            nc.gpsimd.tensor_copy(mask_w[:, 0:P], mask_c[:, 0:P]).then_inc(masks_ready, 1)
            nc.gpsimd.affine_select(out=mask_w[:, P:3 * P], in_=mask_c[:, P:3 * P], compare_op=ALU.is_ge,
                                    fill=NEG, base=WINDOW - 1 - P, pattern=[[1, S]], channel_multiplier=-1)\
                .then_inc(masks_ready, 1)
            pool.wait_ge(rows2_ps, 1)
            nc.gpsimd.memset(y[:, :, :], 0.0).then_inc(y_zero, 1)
            pool.wait_ge(mix_step, 8)
            nc.gpsimd.memset(gate_row[:, :], 0.0).then_inc(gate_zero, 1)

        @block.scalar
        def _(act):
            def split_hi(seg, j, i=0):
                m = seg.of_kind("W", j, i)
                act.wait_ge(raw_in[seg.slot(j)], 16 * seg.loads(j, i))
                act.wait_ge(w_used, used(seg, m - PAIR))
                nc.scalar.copy(pair_hi[seg.pair(j)][:, :], raw[:, seg.slot(j), :]).then_inc(w_hi, 1)

            def split_ki(q):
                act.wait_ge(ki_in, 16 * (q + 1))
                nc.scalar.copy(ki_hi[:, :, :], ki_raw[:, :, :]).then_inc(ki_hi_done, 1)

            def squares(n, b, h, banks):
                if n == 0 and (b or h) or n == 2 and b:
                    act.wait_ge(sq_done, 2 * NB * n + 2 * b + h)
                nc.scalar.activation(ps[:, banks:banks + 2, :].rearrange("p a n -> p (a n)"),
                                     x_sb[:, b, h * 1024:(h + 1) * 1024], ACT.Square,
                                     accum_out=stat[:, 2 * h + b:2 * h + b + 1]).then_inc(sq_done, 1)

            def root(n):
                act.wait_ge(var_done, 2 * (n + 1))
                nc.scalar.activation(stat[:, 6:8], stat[:, 4:6], ACT.Sqrt).then_inc(root_done, 1)

            def normalise(q, n, norm):
                act.wait_ge(rstd_done, norm + 1)
                if later(n):
                    act.wait_ge(xnT_ready, n)
                for b in range(NB):
                    ins = nc.scalar.activation(xn[:, b, :], x_sb[:, b, bass.ds(q * CW, CW)], ACT.Copy,
                                               scale=stat[:, 8 + b:9 + b])
                ins.then_inc(xn_ready, 1)

            act.dma_start(c_rows[:, :], c[0, :].rearrange("(k p) -> k p", p=P)).then_inc(c_in, 16)
            for b in range(NB):
                act.dma_start(x_sb[:, b, :], x[0, b * P:(b + 1) * P, :]).then_inc(x_in[b], 16)
            act.dma_start(b_rows[:, :], b_ada[0, :].rearrange("(k p) -> k p", p=CW)).then_inc(rows_in, 16)
            act.wait_ge(const_ready, 3)
            act.dma_start(rows[0:KT, C_GM, :], g_mix[0, :].rearrange("(k p) -> k p", p=P)).then_inc(rows_in, 16)
            act.dma_start(rows[0:KT, C_GF, :], g_ffn[0, :].rearrange("(k p) -> k p", p=P)).then_inc(rows_in, 16)
            for n in range(3):
                act.dma_start(rows[0:FT, C_W0 + n, :], conv_w[0, n, :].rearrange("(k p) -> k p", p=P))\
                    .then_inc(rows_in, 16)
            act.dma_start(rows[0:FT, C_B, :], conv_b[0, :].rearrange("(k p) -> k p", p=P)).then_inc(rows_in, 16)
            act.dma_start(sink_row[:, :], sinks[0:1, :].to_broadcast([P, HEADS])).then_inc(sink_in, 16)
            act.wait_ge(c_in, 16)
            nc.scalar.activation(c_rows[:, :], c_rows[:, :], ACT.Silu).then_inc(c_act, 1)
            for b in range(NB):
                act.wait_ge(x_in[b], 16)
                for h in range(2):
                    squares(0, b, h, 2 * h)
            root(0)
            normalise(0, 0, 0)
            act.wait_ge(h_ready, 1)
            nc.scalar.copy(op_hi[:, 0:QT, :], h32[:, :, :]).then_inc(h_hi, 1)

            def in_phase(seg, i, q):
                for w, j in enumerate(seg.js("W")):
                    split_hi(seg, j, i)
                    if w == 1:
                        split_ki(q)
                    if w == 2 and seg is IN:
                        normalise(q + 1, q + 1, 0)
                if seg is IN:
                    act.wait_ge(h_ready, q + 2)
                    nc.scalar.copy(op_hi[:, bass.ds((q + 1) * QT, QT), :], h32[:, :, :]).then_inc(h_hi, 1)

            with act.Fori(0, 3) as q:
                in_phase(IN, q, q)
            in_phase(IN3, 0, 3)

            act.wait_ge(ki_added, NQ)
            act.wait_ge(win_added, NQ * NWIN + 2)
            act.dma_start(ki_dup[IDXD:2 * IDXD, :], proj[0:IDXD, T_KI, :]).then_inc(dup_in, 16)
            for t in (T_QB, T_QA):
                nc.scalar.mul(proj[:, t:t + HEADS, :], proj[:, t:t + HEADS, :], HD ** -0.5)\
                    .then_inc(q_scaled, 1)
            for n in range(8):
                act.wait_ge(idx_ps, n + 1)
                if n >= 2:
                    act.wait_ge(idx_sum, 4 * (n - 1))
                w = P * (n // 4 + 1)
                s = n % 2
                nc.scalar.activation(logit[:, s, :, 0:w],
                                     ps[:, 2 * s:2 * s + 2, :].rearrange("p a (h k) -> p (a h) k", h=2)[:, :, 0:w],
                                     ACT.Relu).then_inc(idx_relu, 1)
            def exps(u):
                g, b = divmod(u, NB)
                w = P * (b + 1)
                act.wait_ge(lg_done, u + 1)
                for r in range(4):
                    ins = nc.scalar.activation(logit[:, u % 2, r, 0:w], logit[:, u % 2, r, 0:w], ACT.Exp,
                                               bias=nmx[:, u % 2, r:r + 1], accum_out=den[:, u % 2, r:r + 1])
                if g < KV:
                    ins = nc.scalar.activation(sink_e[:, u % 2, :], sink_d[:, u % 2, :], ACT.Exp)
                ins.then_inc(e_done, 1)

            def outputs(u):
                g, b = divmod(u, NB)
                act.wait_ge(pT_ps, u + 1)
                if u:
                    act.wait_ge(o_ps, u)
                nc.scalar.copy(probT[:, 0:b + 1, :], ps[:, 4:5 + b, :]).then_inc(pT_ready, 1)
                act.wait_ge(o_ps, u + 1)
                t = (HEADS if g < KV else 0) + 4 * (g % KV)
                nc.scalar.copy(op_hi[:, t:t + 4, b * P:(b + 1) * P],
                               ps[:, 6, :].rearrange("p (h q) -> p h q", h=4)).then_inc(o_hi, 1)

            exps(0)
            for u in range(8):
                if u < 7:
                    exps(u + 1)
                outputs(u)
            for n, j in enumerate(MID.js("W")):
                split_hi(MID, j)
                if n >= 4 and n < 8:
                    act.wait_ge(gate_ps, n - 3)
                    nc.scalar.copy(gate_row[:, (n - 4) * CW:(n - 3) * CW], ps[:, GATE_BANK[n - 4], :])\
                        .then_inc(gate_done, 1)
                if n in (13, 14):
                    b = n - 13
                    act.wait_ge(mix_step, 2 * b + 2)
                    squares(1, b, 0, 2 * b)
            for b in range(NB):
                act.wait_ge(mix_step, 6 + 2 * b)
                squares(1, b, 1, 4 + 2 * b)
            root(1)

            def second(q):
                act.wait_ge(h_ready, NQ + q + 1)
                nc.scalar.copy(op_hi[:, QT * q:QT * q + QT, :], h32[:, :, :]).then_inc(h_hi, 1)

            normalise(0, NQ, 1)
            for q in range(NQ):
                if q < NQ - 1:
                    normalise(q + 1, NQ + q + 1, 1)
                second(q)
                split_hi(UP0, 2 * q)
                split_hi(UP0, 2 * q + 1)

            def conv_tail(g):
                for n, t in enumerate(TILE_ORDER):
                    if n == 0:
                        act.wait_ge(w_used, UP_END + 12 * g)
                    if n >= 2:
                        act.wait_ge(conv_step, 2 * CT * g + 2 * (n - 1))
                    nc.scalar.activation(conv[:, t, :], ps[:, t // 2, (t % 2) * S:(t % 2) * S + S], ACT.Identity,
                                         bias=cols[:, C_B, bass.ds(g * CT + t, 1)],
                                         scale=cols[:, C_W2, bass.ds(g * CT + t, 1)]).then_inc(conv_a, 1)
                act.wait_ge(conv_step, 2 * CT * (g + 1))
                nc.scalar.activation(conv[:, :, :], conv[:, :, :], ACT.Silu).then_inc(silu_done, 1)
                act.wait_ge(gu_done, g + 1)
                act.wait_ge(w_used, UP_END + 2 + 12 * g)
                nc.scalar.copy(act_hi[:, :, :], conv[:, :, :]).then_inc(act_hi_done, 1)

            def ffn_body(seg, i, g):
                for n, j in enumerate(seg.js("W")):
                    split_hi(seg, j, i)
                    if n == 1:
                        conv_tail(g - 1)

            with act.Fori(0, FFN_A.times) as i:
                ffn_body(FFN_A, i, i + 1)
            with act.Fori(0, FFN.times) as i:
                ffn_body(FFN, i, i + 1 + FFN_A.times)
            split_hi(LAST, 0)
            split_hi(LAST, 1)
            conv_tail(PASSES - 1)
            split_hi(LAST, 2)
            split_hi(LAST, 3)
            for b in range(NB):
                act.wait_ge(x_step, 2 * b + 2)
                for h in range(2):
                    squares(2, b, h, 4 + 2 * h)
            root(2)

        @block.vector
        def _(dve):
            chained = [0]

            def link(ins):
                chained[0] += 1
                ins.then_inc(chain, 1)
                dve.wait_ge(chain, chained[0])

            def split_lo(seg, j, i=0):
                dve.wait_ge(w_hi, seg.of_kind("W", j, i))
                nc.vector.tensor_tensor(pair_lo[seg.pair(j)][:, :], raw[:, seg.slot(j), :],
                                        pair_hi[seg.pair(j)][:, :].bitcast(F32), ALU.subtract).then_inc(w_split, 1)

            def add_ada(seg, j, i, acc, k, pairs=False):
                n = seg.of_kind("A", j, i)
                dve.wait_ge(raw_in[seg.slot(j)], 16 * seg.loads(j, i))
                for t in range(2 if pairs else 1):
                    if pairs:
                        tile = 2 * k + t
                        w = raw[:, seg.slot(j), t * 1024:(t + 1) * 1024]
                        before = 2 * (n - 1) + t
                        if t:
                            dve.wait_ge(pair_in[seg.slot(j)], 16 * paired_loads(seg, j, i))
                    else:
                        tile = k
                        w = raw[:, seg.slot(j), :]
                        before = PAIRED + n - 1
                    col = silu_c[:, bass.ds(tile, 1)]
                    if isinstance(tile, int) and tile == 0 and seg is not FFN_A:
                        ins = nc.vector.tensor_scalar(acc, w, col, None, ALU.mult)
                    else:
                        dve.wait_ge(ada_sum, before)
                        ins = nc.vector.scalar_tensor_tensor(acc, w, col, acc, ALU.mult, ALU.add)
                    ins.then_inc(ada_sum, 1)

            def paired_loads(seg, j, i):
                if seg is ADA0:
                    return j // RAW + 1
                own = [a for a in seg.js("A") if a % RAW == j % RAW]
                return 2 + own.index(j) + 1 + i * len(own)

            dve.wait_ge(cols_ps, 1)
            nc.vector.tensor_copy(silu_c[:, :], ps[:, 7, 0:KT]).then_inc(cols_ready, 1)
            dve.sem_inc(w_split, RAW)
            dve.wait_ge(cols_ready, 1)
            def rms(n):
                dve.wait_ge(sq_done, 2 * NB * (n + 1))
                nc.vector.tensor_tensor(stat[:, 4:6], stat[:, 0:2], stat[:, 2:4], ALU.add).then_inc(var_done, 1)
                dve.wait_ge(var_done, 2 * n + 1)
                nc.vector.tensor_scalar(stat[:, 4:6], stat[:, 4:6], 1.0 / D, EPS, ALU.mult, ALU.add)\
                    .then_inc(var_done, 1)
                dve.wait_ge(root_done, n + 1)
                nc.vector.reciprocal(stat[:, 8:10], stat[:, 6:8]).then_inc(rstd_done, 1)

            def mod_columns(q, n):
                dve.wait_ge(mod_ps, n + 1)
                sc, sh = (b_cols[:, :, bass.ds(v * NQ + q, 1)].rearrange("p t a -> p (t a)")
                          for v in (SCALE1, SHIFT1))
                to_s, to_b = (m[:, bass.ds(q * QT, QT)] for m in (mod_s, mod_b))
                nc.vector.tensor_tensor(to_s, ps[:, 7, QT:2 * QT], sc, ALU.add).then_inc(mod_done, 1)
                nc.vector.tensor_tensor(to_b, ps[:, 7, 0:QT], sh, ALU.add).then_inc(mod_done, 1)
                dve.wait_ge(mod_done, 3 * n + 2)
                nc.vector.scalar_tensor_tensor(to_s, to_s, 1.0, cols[:, C_GM, bass.ds(q * QT, QT)],
                                               ALU.add, ALU.mult).then_inc(mod_done, 1)
                dve.wait_ge(mod_done, 3 * n + 3)

            def modulate(q, n, tile, free_after=None):
                dve.wait_ge(xnT_ready, n + 1)
                if later(n):
                    dve.wait_ge(h_lo, n)
                for t in range(QT):
                    ins = nc.vector.tensor_scalar(h32[:, t, :], ps[:, 5 + t // 2, (t % 2) * S:(t % 2) * S + S],
                                                  mod_s[:, bass.ds(q * QT + t, 1)], mod_b[:, bass.ds(q * QT + t, 1)],
                                                  ALU.mult, ALU.add)
                ins.then_inc(h_ready, 1)
                dve.wait_ge(h_hi, n + 1)
                dve.wait_ge(h_ready, n + 1)
                nc.vector.tensor_tensor(op_lo[:, bass.ds(tile, QT), :], h32[:, :, :],
                                        op_hi[:, bass.ds(tile, QT), :].bitcast(F32), ALU.subtract).then_inc(h_lo, 1)

            for j in range(8):
                add_ada(ADA0, j, 0, ada_acc[:, :, :].rearrange("p v n -> p (v n)"), j, True)
                if j == 2:
                    dve.wait_ge(cols_ps, 2)
                    nc.vector.tensor_copy(cols[:, :, :], ps[:, 6, 0:6 * 44].rearrange("p (a n) -> p a n", a=6))\
                        .then_inc(cols_ready, 1)
                    nc.vector.tensor_copy(b_cols[:, :, :], ps[:, 6, 6 * 44:6 * 44 + QT * 24]
                                          .rearrange("p (t n) -> p t n", t=QT)).then_inc(cols_ready, 1)
                if j == 4:
                    rms(0)
            dve.wait_ge(cols_ready, 3)
            nc.vector.memset(ps[:, 0:4, :], 0.0).then_inc(bank_zero, 1)
            mod_columns(0, 0)
            modulate(0, 0, 0)
            dve.wait_ge(proj_zero, 1)
            dve.wait_ge(bank_zero, 1)

            def add_window(v, w):
                dve.wait_ge(w_used, used(IN, v))
                b = 2 * (w % 2)
                dst = proj[:, WIN_TILE[w]:WIN_TILE[w] + CT, :]
                nc.vector.tensor_tensor(dst, dst, ps[:, b:b + 2, :].rearrange("p a (t n) -> p (a t) n", t=2),
                                        ALU.add).then_inc(win_added, 1)

            def in_phase(seg, i, q):
                a, w = 0, 0
                for j, kind in enumerate(seg.kinds):
                    if kind == "A":
                        if seg is IN:
                            add_ada(seg, j, i, ada_acc[:, :, :].rearrange("p v n -> p (v n)"), a, True)
                        else:
                            add_ada(seg, j, i, gate_row[:, :], a)
                        a += 1
                        continue
                    split_lo(seg, j, i)
                    if w == 1:
                        dve.wait_ge(ki_hi_done, q + 1)
                        nc.vector.tensor_tensor(ki_lo[:, :, :], ki_raw[:, :, :], ki_hi[:, :, :].bitcast(F32),
                                                ALU.subtract).then_inc(ki_split, 1)
                    add_window(q * NWIN + w - 1, (w - 2) % NWIN)
                    if w == 5:
                        dve.wait_ge(ki_used, q + 1)
                        nc.vector.tensor_tensor(proj[0:SMALL, T_KI, :], proj[0:SMALL, T_KI, :],
                                                ps[0:SMALL, 4, 0:S], ALU.add).then_inc(ki_added, 1)
                    w += 1
                if seg is IN:
                    mod_columns(q + 1, q + 1)
                    modulate(q + 1, q + 1, (q + 1) * QT)

            with dve.Fori(0, 3) as q:
                in_phase(IN, q, q)
            in_phase(IN3, 0, 3)
            for w in (6, 7):
                add_window(3 * NWIN + w + 1, w)

            dve.wait_ge(masks_ready, 1)
            for n in range(NB):
                dve.wait_ge(vT_ps, 1)
                ins = nc.vector.tensor_copy(v_tok[:, n, :, :], ps[:, 4 + n, :].rearrange("p (a d) -> p a d", a=4))
            ins.then_inc(v_ready, 1)
            nc.vector.tensor_scalar(w_tok[:, :, :], ps[:, 6, 0:2 * P].rearrange("p (b n) -> p b n", b=NB),
                                    (IDXD ** -0.5) * (IDXH ** -0.5), None, ALU.mult).then_inc(v_ready, 1)
            dve.wait_ge(v_ready, 2)

            mid_a = MID.js("A")

            for n in range(8):
                blk, hh = divmod(n, 4)
                w = P * (blk + 1)
                dve.wait_ge(idx_relu, n + 1)
                for r in range(4):
                    head = 4 * hh + (0, 2, 1, 3)[r]
                    wcol = w_tok[:, blk, IDXD + head:IDXD + head + 1]
                    if hh == 0 and r == 0:
                        ins = nc.vector.tensor_scalar(score[:, blk, 0:w], logit[:, n % 2, r, 0:w], wcol, None,
                                                      ALU.mult)
                    else:
                        ins = nc.vector.scalar_tensor_tensor(score[:, blk, 0:w], logit[:, n % 2, r, 0:w], wcol,
                                                             score[:, blk, 0:w], ALU.mult, ALU.add)
                    ins.then_inc(idx_sum, 1)
                    dve.wait_ge(idx_sum, 4 * n + r + 1)
                if n < 4:
                    add_ada(MID, mid_a[n], 0, gate_row[:, :], 8 + n)

            dve.wait_ge(masks_ready, 6)
            for blk in range(NB):
                w = P * (blk + 1)
                m = slice(blk * P, blk * P + w)
                link(nc.vector.tensor_tensor(score[:, blk, 0:w], score[:, blk, 0:w], mask_c[:, m], ALU.add))
                for _ in range(TOPK // 8):
                    link(nc.vector.max(top8[:, :], score[:, blk, 0:w]))
                    link(nc.vector.match_replace(score[:, blk, 0:w], top8[:, :], score[:, blk, 0:w], TAKEN))
                link(nc.vector.tensor_scalar(mask_a[:, m], score[:, blk, 0:w], TAKEN / 2, NEG, ALU.is_gt, ALU.mult))
                link(nc.vector.tensor_tensor(mask_a[:, m], mask_a[:, m], mask_c[:, m], ALU.min))

            dve.wait_ge(sink_in, 16)

            def front(u):
                g, b = divmod(u, NB)
                w = P * (b + 1)
                m = slice(b * P, b * P + w)
                mask = mask_w if g < KV else mask_a
                dve.wait_ge(lg_ps, u + 1)
                if u >= 2:
                    dve.wait_ge(pT_ps, u - 1)
                for r in range(4):
                    slope = SLOPE[2 * (4 * (g % KV) + r) + (1 if g < KV else 0)]
                    link(nc.vector.scalar_tensor_tensor(bias[:, r % 2, 0:w], dist[:, m], -slope, mask[:, m],
                                                        ALU.mult, ALU.add))
                    head = 4 * (g % KV) + r
                    least = sink_row[:, head:head + 1] if g < KV else -3e38
                    ins = nc.vector.tensor_tensor_reduce(logit[:, u % 2, r, 0:w],
                                                   ps[:, 2 * (u % 2) + r // 2, (r % 2) * S:(r % 2) * S + w],
                                                   bias[:, r % 2, 0:w], 1.0, least, ALU.add, ALU.max,
                                                   mx[:, u % 2, r:r + 1])
                link(ins)
                ins = nc.vector.tensor_scalar(nmx[:, u % 2, :], mx[:, u % 2, :], -1.0, None, ALU.mult)
                if g < KV:
                    ins = nc.vector.tensor_tensor(sink_d[:, u % 2, :], sink_row[:, 4 * g:4 * g + 4],
                                                  mx[:, u % 2, :], ALU.subtract)
                ins.then_inc(lg_done, 1)

            def back(u):
                g, b = divmod(u, NB)
                w = P * (b + 1)
                dve.wait_ge(e_done, u + 1)
                if g < KV:
                    link(nc.vector.tensor_tensor(den[:, u % 2, :], den[:, u % 2, :], sink_e[:, u % 2, :], ALU.add))
                link(nc.vector.reciprocal(rden[:, u % 2, :], den[:, u % 2, :]))
                for r in range(4):
                    ins = nc.vector.tensor_scalar(logit[:, u % 2, r, 0:w], logit[:, u % 2, r, 0:w],
                                                  rden[:, u % 2, r:r + 1], None, ALU.mult)
                ins.then_inc(p_ready, 1)

            def tail(u):
                g, b = divmod(u, NB)
                t = (HEADS if g < KV else 0) + 4 * (g % KV)
                dve.wait_ge(o_hi, u + 1)
                nc.vector.tensor_tensor(op_lo[:, t:t + 4, b * P:(b + 1) * P],
                                        ps[:, 6, :].rearrange("p (h q) -> p h q", h=4),
                                        op_hi[:, t:t + 4, b * P:(b + 1) * P].bitcast(F32), ALU.subtract)\
                    .then_inc(o_lo, 1)

            front(0)
            for u in range(8):
                if u < 7:
                    front(u + 1)
                back(u)
                if u:
                    tail(u - 1)
            tail(7)

            def add_mix(h):
                dve.wait_ge(w_used, used(MID, MID.of_kind("W", MID.js("W")[8 * h + 7])))
                if h == 0:
                    dve.wait_ge(gate_done, NQ)
                for b in range(NB):
                    bank = 4 * h + 2 * b
                    step = 4 * h + 2 * b
                    mixed = ps[:, bank:bank + 2, :].rearrange("p a n -> p (a n)")
                    tmp = h32[:, :, :].rearrange("p a n -> p (a n)")
                    nc.vector.tensor_tensor(tmp, mixed, gate_row[:, h * 1024:(h + 1) * 1024], ALU.mult)\
                        .then_inc(mix_step, 1)
                    dve.wait_ge(mix_step, step + 1)
                    dst = x_sb[:, b, h * 1024:(h + 1) * 1024]
                    nc.vector.tensor_tensor(dst, dst, tmp, ALU.add).then_inc(mix_step, 1)
                    dve.wait_ge(mix_step, step + 2)

            def mod2(vec, bank, dst):
                n = 0 if vec == SCALE2 else 1
                if n == 0:
                    dve.wait_ge(q_used, KT)
                else:
                    dve.wait_ge(rows2_ps, 1)
                nc.vector.tensor_copy(xn[:, n, :], ps[:, bank, :]).then_inc(rows2_done, 1)

            def mod2_columns(vec, bank, dst):
                n = 0 if vec == SCALE2 else 1
                dve.wait_ge(mod2_ps, n + 1)
                to = dst[:, :].rearrange("p (j t) -> p t j", j=NQ)
                nc.vector.tensor_tensor(to, ps[:, bank, :].rearrange("p (t j x) -> p t j x", t=QT, j=NQ)[:, :, :, 0],
                                        b_cols[:, :, vec * NQ:vec * NQ + NQ], ALU.add).then_inc(mod2_done, 1)
                dve.wait_ge(mod2_done, n + 1)

            a, w = 4, 0
            shift_sum = y[:, 1, :]
            for j in range(20, len(MID.kinds)):
                if MID.kinds[j] == "A":
                    if a < 8:
                        add_ada(MID, j, 0, gate_row[:, :], 8 + a)
                    else:
                        add_ada(MID, j, 0, shift_sum, a - 8)
                    a += 1
                    continue
                split_lo(MID, j)
                if w == 3:
                    mod2(SCALE2, 7, mod_s)
                if w == 6:
                    mod2_columns(SCALE2, 4, mod_s)
                    link(nc.vector.scalar_tensor_tensor(mod_s[:, :], mod_s[:, :], 1.0, cols[:, C_GF, 0:KT],
                                                        ALU.add, ALU.mult))
                if w == 11:
                    add_mix(0)
                w += 1
            mod2(SHIFT2, 0, mod_b)
            mod2_columns(SHIFT2, 1, mod_b)
            add_mix(1)
            rms(1)
            modulate(0, NQ, 0)
            for q in range(NQ):
                split_lo(UP0, 2 * q)
                split_lo(UP0, 2 * q + 1)
                if q < NQ - 1:
                    modulate(q + 1, NQ + q + 1, QT * (q + 1))

            def conv_taps(g):
                for n, t in enumerate(TILE_ORDER):
                    dve.wait_ge(conv_a, g * CT + n + 1)
                    for lag, tap in ((1, C_W1), (2, C_W0)):
                        gate_ps_t = ps[:, t // 2, (t % 2) * S:(t % 2) * S + S - lag]
                        ins = nc.vector.scalar_tensor_tensor(conv[:, t, lag:S], gate_ps_t,
                                                             cols[:, tap, bass.ds(g * CT + t, 1)],
                                                             conv[:, t, lag:S], ALU.mult, ALU.add)
                        ins.then_inc(conv_step, 1)
                        dve.wait_ge(conv_step, g * 2 * CT + 2 * n + lag)
                dve.wait_ge(silu_done, g + 1)
                nc.vector.tensor_tensor(conv[:, :, :], conv[:, :, :],
                                        ps[:, 2:4, :].rearrange("p a (t n) -> p (a t) n", t=2), ALU.mult)\
                    .then_inc(gu_done, 1)
                dve.wait_ge(act_hi_done, g + 1)
                dve.wait_ge(gu_done, g + 1)
                nc.vector.tensor_tensor(act_lo[:, :, :], conv[:, :, :], act_hi[:, :, :].bitcast(F32),
                                        ALU.subtract).then_inc(act_split, 1)

            def add_y(h, count):
                dve.wait_ge(w_used, count)
                dst = y[:, :, h * 1024:(h + 1) * 1024]
                nc.vector.tensor_tensor(dst, dst, ps[:, 4:8, :].rearrange("p (b a) n -> p b (a n)", b=NB),
                                        ALU.add).then_inc(y_added, 1)

            def ffn_body(seg, i, g):
                a = 0
                w_js = seg.js("W")
                w = 0
                for j, kind in enumerate(seg.kinds):
                    if kind == "A":
                        add_ada(seg, j, i, gate_row[:, :], i * QT + a)
                        a += 1
                        continue
                    split_lo(seg, j, i)
                    if w == 1:
                        conv_taps(g - 1)
                    if w == 3:
                        add_y(1, used(seg, seg.of_kind("W", w_js[0], i) - 1))
                    if w == 8:
                        add_y(0, used(seg, seg.of_kind("W", w_js[5], i)))
                    w += 1

            link(nc.vector.memset(ps[:, 4:8, :], 0.0))
            dve.wait_ge(y_zero, 1)
            dve.wait_ge(gate_zero, 1)
            with dve.Fori(0, FFN_A.times) as i:
                ffn_body(FFN_A, i, i + 1)
            with dve.Fori(0, FFN.times) as i:
                ffn_body(FFN, i, i + 1 + FFN_A.times)
            split_lo(LAST, 0)
            split_lo(LAST, 1)
            conv_taps(PASSES - 1)
            add_y(1, used(LAST, LAST.of_kind("W", 0) - 1))
            split_lo(LAST, 2)
            split_lo(LAST, 3)
            add_y(0, used(LAST, LAST.of_kind("W", 1)))
            add_y(1, used(LAST, LAST.of_kind("W", 3)))
            dve.wait_ge(gate2_ps, 1)
            dve.wait_ge(y_added, 2 * PASSES + 1)
            for b in range(NB):
                yb = y[:, b, :]
                nc.vector.tensor_tensor(yb, yb, ps[:, 0:4, :].rearrange("p a n -> p (a n)"), ALU.mult)\
                    .then_inc(x_step, 1)
                dve.wait_ge(x_step, 2 * b + 1)
                nc.vector.tensor_tensor(x_sb[:, b, :], x_sb[:, b, :], yb, ALU.add).then_inc(x_step, 1)
            rms(2)
            dve.wait_ge(rstd_done, 3)
            dve.wait_ge(gf_in, 16)
            for b in range(NB):
                nc.vector.scalar_tensor_tensor(raw[:, 2 + b, :], x_sb[:, b, :], stat[:, 8 + b:9 + b],
                                               raw[:, 0, :], ALU.mult, ALU.mult).then_inc(y_ready, 1)

        @block.tensor
        def _(pe):
            def three(dst, s_hi, s_lo, m_hi, m_lo, first, last, more=True):
                nc.tensor.matmul(dst, s_hi, m_hi, start=first, stop=False, skip_group_check=True)
                nc.tensor.matmul(dst, s_hi, m_lo, start=False, stop=False, skip_group_check=True)
                return nc.tensor.matmul(dst, s_lo, m_hi, start=False, stop=last, skip_group_check=True)

            pe.wait_ge(const_ready, 2)
            pe.wait_ge(c_act, 1)
            nc.tensor.transpose(ps[:, 7, 0:KT], c_rows[:, :], ident[0:KT, 0:KT]).then_inc(cols_ps, 1)
            pe.wait_ge(const_ready, 4)
            pe.wait_ge(rows_in, 16 * 7)
            for n in range(6):
                nc.tensor.transpose(ps[:, 6, n * 44:(n + 1) * 44], rows[0:44, n, :], ident[0:44, 0:44])
            for t in range(QT):
                mm = nc.tensor.transpose(ps[:, 6, 6 * 44 + t * 24:6 * 44 + (t + 1) * 24],
                                         b_rows[:, t * P:(t + 1) * P], ident[0:24, 0:24])
            mm.then_inc(cols_ps, 1)
            pe.wait_ge(cols_ready, 3)
            pe.sem_inc(w_used, PAIR)

            def turn_xn(n):
                pe.wait_ge(xn_ready, n + 1)
                if later(n):
                    pe.wait_ge(h_ready, n)
                for t in range(QT):
                    for b in range(NB):
                        mm = nc.tensor.transpose(ps[:, 5 + t // 2, (t % 2) * S + b * P:(t % 2) * S + (b + 1) * P],
                                                 xn[:, b, t * P:(t + 1) * P], ident[:, :])
                mm.then_inc(xnT_ready, 1)

            def reduce_mods(n):
                pe.wait_ge(ada_sum, 16 * (n + 1))
                if later(n):
                    pe.wait_ge(mod_done, 3 * n)
                for half in range(2):
                    for t in range(QT):
                        mm = nc.tensor.matmul(ps[:, 7, half * QT + t:half * QT + t + 1],
                                              ada_acc[:, half, t * P:(t + 1) * P], ones[:, 0:1],
                                              start=True, stop=True, skip_group_check=True)
                mm.then_inc(mod_ps, 1)

            turn_xn(0)
            reduce_mods(0)

            def in_window(seg, j, i, q, w):
                pe.wait_ge(win_added, q * NWIN + w + 1)
                pe.wait_ge(w_split, split(seg.of_kind("W", j, i)))
                hi, lo = pair_hi[seg.pair(j)], pair_lo[seg.pair(j)]
                for k in range(QT):
                    for t in range(CT):
                        s = slice(k * CW + t * P, k * CW + (t + 1) * P)
                        mm = three(ps[:, 2 * (w % 2) + t // 2, (t % 2) * S:(t % 2) * S + S],
                                   hi[:, s], lo[:, s], op(op_hi, q, k), op(op_lo, q, k),
                                   k == 0 and t % 2 == 0, k == QT - 1)
                mm.then_inc(w_used, 1)

            def op(half, q, k):
                return half[:, bass.ds(q * QT + k, 1), :].rearrange("p a n -> p (a n)")

            def in_small(q):
                pe.wait_ge(ki_split, q + 1)
                for k in range(QT):
                    mm = three(ps[0:SMALL, 4, 0:S], ki_hi[:, k, :], ki_lo[:, k, :], op(op_hi, q, k), op(op_lo, q, k),
                               k == 0, k == QT - 1)
                mm.then_inc(ki_used, 1)

            def in_phase(seg, i, q):
                pe.wait_ge(h_lo, q + 1)
                for w, j in enumerate(seg.js("W")):
                    in_window(seg, j, i, q, w)
                    if w == 2:
                        in_small(q)
                    if w == 3 and seg is IN:
                        turn_xn(q + 1)
                    if w == 5 and seg is IN:
                        reduce_mods(q + 1)

            with pe.Fori(0, 3) as q:
                in_phase(IN, q, q)
            in_phase(IN3, 0, 3)

            pe.wait_ge(win_added, NQ * NWIN + 2)
            pe.wait_ge(ki_added, NQ)
            for b in range(NB):
                for n, t in enumerate((T_VB, T_VB + 1, T_VA, T_VA + 1)):
                    nc.tensor.transpose(ps[:, 4 + b, n * P:(n + 1) * P], proj[:, t, b * P:(b + 1) * P], ident[:, :])
            for b in range(NB):
                mm = nc.tensor.transpose(ps[:, 6, b * P:(b + 1) * P], proj[:, T_KI, b * P:(b + 1) * P], ident[:, :])
            mm.then_inc(vT_ps, 1)

            scale2_js = MID.js("Q")

            def scale2(n):
                j = scale2_js[n]
                pe.wait_ge(raw_in[MID.slot(j)], 16 * MID.loads(j))
                for m in range(NQ):
                    mm = nc.tensor.matmul(ps[32 * m:32 * m + 32, 7, :], silu_c[:, n:n + 1].to_broadcast([P, 32]),
                                          raw[:, MID.slot(j), m * CW:(m + 1) * CW],
                                          start=(n == 0), stop=(n == KT - 1), skip_group_check=True)
                mm.then_inc(q_used, 1)

            pe.wait_ge(dup_in, 16)
            for n in range(8):
                blk, hh = divmod(n, 4)
                w = P * (blk + 1)
                if n >= 2:
                    pe.wait_ge(idx_relu, n - 1)
                for odd in range(2):
                    rows_ = slice(IDXD * odd, IDXD * odd + IDXD)
                    keys = ki_dup[rows_, 0:w] if odd else proj[rows_, T_KI, 0:w]
                    for m in range(2):
                        t = T_QI + 2 * hh + m
                        mm = nc.tensor.matmul(ps[:, 2 * (n % 2) + odd, m * S:m * S + w],
                                              proj[rows_, t, blk * P:(blk + 1) * P], keys, start=True, stop=True)
                mm.then_inc(idx_ps, 1)
                scale2(n)

            def logits(u):
                g, b = divmod(u, NB)
                w = P * (b + 1)
                if u >= 2:
                    pe.wait_ge(lg_done, u - 1)
                elif u == 0:
                    pe.wait_ge(idx_relu, 8)
                    pe.wait_ge(q_scaled, 2)
                q0, k0 = (T_QB, T_KB) if g < KV else (T_QA, T_KA)
                for r in range(4):
                    mm = nc.tensor.matmul(ps[:, 2 * (u % 2) + r // 2, (r % 2) * S:(r % 2) * S + w],
                                          proj[:, q0 + 4 * (g % KV) + r, b * P:(b + 1) * P],
                                          proj[:, k0 + g % KV, 0:w], start=True, stop=True)
                mm.then_inc(lg_ps, 1)

            def values(u):
                g, b = divmod(u, NB)
                pe.wait_ge(p_ready, u + 1)
                pe.wait_ge(v_ready, 2)
                if u:
                    pe.wait_ge(pT_ready, u)
                for kt in range(b + 1):
                    for r in range(4):
                        mm = nc.tensor.transpose(ps[:, 4 + kt, r * P:(r + 1) * P],
                                                 logit[:, u % 2, r, kt * P:(kt + 1) * P], ident[:, :])
                mm.then_inc(pT_ps, 1)
                pe.wait_ge(pT_ready, u + 1)
                if u:
                    pe.wait_ge(o_lo, u)
                for kt in range(b + 1):
                    mm = nc.tensor.matmul(ps[:, 6, :], v_tok[:, kt, g, :], probT[:, kt, :],
                                          start=(kt == 0), stop=(kt == b))
                mm.then_inc(o_ps, 1)

            logits(0)
            logits(1)
            for u in range(8):
                values(u)
                if u < 6:
                    logits(u + 2)
                scale2(8 + u)

            pe.wait_ge(o_lo, 8)

            def down_chunk(seg, j, i, s_hi, s_lo, tile, bank, first, last):
                pe.wait_ge(w_split, split(seg.of_kind("W", j, i)))
                hi, lo = pair_hi[seg.pair(j)], pair_lo[seg.pair(j)]
                for k in range(2):
                    for b in range(NB):
                        tok = slice(b * P, (b + 1) * P)
                        for n, (st, w) in enumerate(((s_hi, hi), (s_hi, lo), (s_lo, hi))):
                            for a in range(2):
                                mm = nc.tensor.matmul(ps[:, bank + 2 * b + a, :], st[:, tile + k, tok],
                                                      w[:, k * 1024 + a * CW:k * 1024 + (a + 1) * CW],
                                                      start=(first and k == 0 and n == 0),
                                                      stop=(last and k == 1 and n == 2), skip_group_check=True)
                mm.then_inc(w_used, 1)

            def to_rows(total, bank):
                for m in range(NQ):
                    mm = nc.tensor.matmul(ps[32 * m:32 * m + 32, bank, :], ones[:, 0:32],
                                          total[:, m * CW:(m + 1) * CW], start=True, stop=True)
                mm.then_inc(rows2_ps, 1)

            def to_columns(n, bank):
                pe.wait_ge(rows2_done, n + 1)
                for t in range(QT):
                    mm = nc.tensor.transpose(ps[:, bank, t * P:(t + 1) * P], xn[:, n, t * P:(t + 1) * P],
                                             ident[:, :])
                mm.then_inc(mod2_ps, 1)

            for n, j in enumerate(MID.js("W")):
                h, pr = divmod(n, 8)
                if n == 8:
                    pe.wait_ge(gate_done, NQ)
                    pe.wait_ge(mod2_done, 1)
                down_chunk(MID, j, 0, op_hi, op_lo, 2 * pr, 4 * h, pr == 0, pr == 7)
                if 3 <= n < 7:
                    m = n - 3
                    pe.wait_ge(ada_sum, sums(IN3.before["A"] + KT))
                    if m >= 2:
                        pe.wait_ge(gate_done, m - 1)
                    nc.tensor.matmul(ps[:, GATE_BANK[m], :], ones[:, :], gate_row[:, m * CW:(m + 1) * CW],
                                     start=True, stop=False)
                    nc.tensor.matmul(ps[:, GATE_BANK[m], :],
                                     ident[0:24, GATE1 * NQ + m:GATE1 * NQ + m + 1].to_broadcast([24, P]),
                                     b_rows[:, :], start=False, stop=True).then_inc(gate_ps, 1)
                if n == 4:
                    to_columns(0, 4)
                if n == 14:
                    pe.wait_ge(sq_done, 2 * NB + 2)
                    pe.wait_ge(ada_sum, sums(MID.of_kind("A", len(MID.kinds) - 1)))
                    to_rows(y[:, 1, :], 0)
            to_columns(1, 1)

            def up_chunk(seg, j, i, n, inc=1):
                pe.wait_ge(w_split, split(seg.of_kind("W", j, i)))
                hi, lo = pair_hi[seg.pair(j)], pair_lo[seg.pair(j)]
                q = n // 2
                for k in range(QT):
                    for t in range(CT):
                        cs = slice(k * CW + t * P, k * CW + (t + 1) * P)
                        mm = three(ps[:, 2 * (n % 2) + t // 2, (t % 2) * S:(t % 2) * S + S],
                                   hi[:, cs], lo[:, cs], op_hi[:, q * QT + k, :], op_lo[:, q * QT + k, :],
                                   q == 0 and k == 0 and t % 2 == 0, q == NQ - 1 and k == QT - 1)
                mm.then_inc(w_used, inc)

            turn_xn(NQ)
            turn_xn(NQ + 1)
            for n in range(8):
                if n in (1, 3):
                    turn_xn(NQ + 2 + n // 2)
                pe.wait_ge(h_lo, NQ + n // 2 + 1)
                up_chunk(UP0, n, 0, n, 3 if n == 7 else 1)

            def ffn_body(seg, i, g):
                js = seg.js("W")
                pe.wait_ge(gu_done, g)
                for n in range(4):
                    up_chunk(seg, js[n], i, n)
                pe.wait_ge(act_split, g)
                pe.wait_ge(y_added, 2 * g - 1)
                for n in range(2):
                    down_chunk(seg, js[4 + n], i, act_hi, act_lo, 2 * n, 4, n == 0, n == 1)
                for n in range(4, 8):
                    up_chunk(seg, js[2 + n], i, n)
                pe.wait_ge(y_added, 2 * g)
                for n in range(2):
                    down_chunk(seg, js[10 + n], i, act_hi, act_lo, 2 * n, 4, n == 0, n == 1)

            with pe.Fori(0, FFN_A.times) as i:
                ffn_body(FFN_A, i, i + 1)
            with pe.Fori(0, FFN.times) as i:
                ffn_body(FFN, i, i + 1 + FFN_A.times)
            pe.wait_ge(act_split, PASSES)
            pe.wait_ge(y_added, 2 * PASSES - 1)
            for n in range(2):
                down_chunk(LAST, n, 0, act_hi, act_lo, 2 * n, 4, n == 0, n == 1)
            pe.wait_ge(ada_sum, sums(FFN.before["A"]))
            for n in range(NQ):
                nc.tensor.matmul(ps[:, n, :], ones[:, :], gate_row[:, n * CW:(n + 1) * CW], start=True, stop=False)
                mm = nc.tensor.matmul(ps[:, n, :],
                                      ident[0:24, GATE2 * NQ + n:GATE2 * NQ + n + 1].to_broadcast([24, P]),
                                      b_rows[:, :], start=False, stop=True)
            mm.then_inc(gate2_ps, 1)
            pe.wait_ge(y_added, 2 * PASSES)
            for n in range(2):
                down_chunk(LAST, 2 + n, 0, act_hi, act_lo, 2 * n, 4, n == 0, n == 1)


_INS = ['x', 'c', 'w_ada', 'b_ada', 'g_mix', 'w_in', 'sinks', 'w_o', 'g_ffn', 'w_gate', 'w_up', 'conv_w',
        'conv_b', 'w_down', 'g_final']
_OUTS = [((1, S, D), 'float32')]


def kernel(**inputs):
    import numpy as _np
    import concourse.bacc as _bacc
    from concourse import mybir as _mybir
    from concourse.bass_utils import run_bass_kernel_spmd as _run

    nc = _bacc.Bacc("TRN2", target_bir_lowering=False, num_devices=1)
    arrays, args = {}, []
    for name in _INS:
        a = _np.ascontiguousarray(inputs[name])
        arrays[f"in_{name}_dram"] = a
        args.append(nc.dram_tensor(f"in_{name}_dram", a.shape, _mybir.dt.from_np(a.dtype), kind="ExternalInput").ap())
    for i, (shape, dtype) in enumerate(_OUTS):
        dt = _mybir.dt.from_np(_np.dtype(dtype))
        args.append(nc.dram_tensor(f"out_{i}_dram", shape, dt, kind="ExternalOutput").ap())
    program(nc, *args)
    r = _run(nc, [arrays], core_ids=[0])
    got = tuple(r.results[0][f"out_{i}_dram"] for i in range(len(_OUTS)))
    return got[0]
```

```python
from contextlib import ExitStack

import concourse.bass as bass
from concourse import mybir

ALU = mybir.AluOpType
ACT = mybir.ActivationFunctionType
AX = mybir.AxisListType
F32 = mybir.dt.float32
F32R = mybir.dt.float32r

P = 128
D = 2048
S = 256
HD = 128
KT = D // P
NB = S // P
HEADS = 8
KV = 2
IDXH = 16
IDXD = 64
TOPK = min(256, S // 4)
WINDOW = 128
F = 11 * D // 4
FT = F // P
EPS = 1e-6
NEG = -1e30
TAKEN = -3e38
NQ = 4
QT = KT // NQ
CW = 512
CT = CW // P
RAW = 4
PAIR = 4
PASSES = F // CW
SMALL = IDXD + IDXH
IN_W = 2 * (HEADS + 2 * KV) * HD + IDXH * IDXD + SMALL
T_QA, T_KA, T_VA, T_QI, T_KI, T_QB, T_KB, T_VB = 0, 8, 10, 12, 20, 21, 29, 31
NT = 33
TILE_ORDER = [0, 2, 1, 3]
WIN_COL = [0, 512, 1024, 1536, 2048, 2640, 3152, 3664]
WIN_TILE = [0, 4, 8, 12, 16, 21, 25, 29]
SMALL_COL = 2560
NWIN = len(WIN_COL)
SLOPE = [2.0 ** (-8.0 * (n + 1) / (2 * HEADS)) for n in range(2 * HEADS)]
SHIFT1, SCALE1, GATE1, SHIFT2, SCALE2, GATE2 = range(6)

SEG_ADA0 = ("A" * 8 + "W", 1)
SEG_IN = ("AW" * 6 + "AAWW", 3)
SEG_IN3 = ("AW" * 6 + "AAW", 1)
INDEX_KINDS = ["QA", "A"] * 3 + ["Q", ""]
UNIT_KINDS = ["Q" + ("A" if u < 6 else "W") for u in range(8)]
SEG_MID = ("".join(INDEX_KINDS) + "Q" * 4 + "".join(UNIT_KINDS) + "AW" * 12 + "WW", 1)
SEG_UP0 = ("W" * 8, 1)
SEG_FFN_1 = ("WWWAWWWAWWWAWWWA", 1)
SEG_FFN_A = ("WWWAWWWAWWWAWWWA", 3)
SEG_FFN = ("W" * 12, 6)
SEG_LAST = ("W" * 4, 1)
SEGS = [SEG_ADA0, SEG_IN, SEG_IN3, SEG_MID, SEG_UP0, SEG_FFN_1, SEG_FFN_A, SEG_FFN, SEG_LAST]


def later(n):
    return not (isinstance(n, int) and n == 0)


MIX_PAIRS = [4, 5, 6, 7, 0, 1, 2, 3]
UP_AHEAD = 3
GATE_BANK = [5, 6, 5, 6]


class Stream:

    def __init__(self, index):
        self.kinds, self.times = SEGS[index]
        self.before = {k: sum(s.count(k) * t for s, t in SEGS[:index]) for k in "AWQ"}
        self.start = sum(len(s) * t for s, t in SEGS[:index])

    def number(self, j, i=0):
        return self.start + i * len(self.kinds) + j

    def slot(self, j):
        return (self.start + j) % RAW

    def loads(self, j, i=0):
        return (self.start + j) // RAW + 1 + i * (len(self.kinds) // RAW)

    def of_kind(self, k, j, i=0):
        return self.before[k] + i * self.kinds.count(k) + self.kinds[:j + 1].count(k)

    def pair(self, j):
        return (self.of_kind("W", j) - 1) % PAIR

    def js(self, k):
        return [j for j, x in enumerate(self.kinds) if x == k]


ADA0, IN, IN3, MID, UP0, FFN_1, FFN_A, FFN, LAST = (Stream(n) for n in range(len(SEGS)))


def program(nc, x, c, w_ada, b_ada, g_mix, w_in, sinks, w_o, g_ffn, w_gate, w_up, conv_w, conv_b,
            w_down, g_final, out):
    ctx = ExitStack()
    with ctx:
        def sb(name, shape, dt=F32):
            return ctx.enter_context(nc.sbuf_tensor(name, shape, dt))

        def sem(name):
            return ctx.enter_context(nc.semaphore(name))

        x_sb = sb("x_sb", [P, NB, D])
        op_hi = sb("op_hi", [P, KT, S], F32R)
        op_lo = sb("op_lo", [P, KT, S], F32R)
        raw = sb("raw", [P, RAW, 2048])
        pair_hi = [None] * PAIR
        pair_lo = [None] * PAIR
        for n in range(2):
            pair_hi[n] = sb(f"pair_hi{n}", [P, 2048], F32R)
            pair_lo[n] = sb(f"pair_lo{n}", [P, 2048], F32R)
        h32 = sb("h32", [P, QT, S])
        xn = sb("xn", [P, NB, CW])
        ada_acc = sb("ada_acc", [P, 2, CW])
        with nc.sbuf_tensor("rows", [44, 6, P], F32) as rows:
            pass
        gate_row = sb("gate_row", [P, D])
        ki_raw = sb("ki_raw", [P, QT, SMALL])
        ki_hi = sb("ki_hi", [P, QT, SMALL], F32R)
        ki_lo = sb("ki_lo", [P, QT, SMALL], F32R)
        ident = sb("ident", [P, P])
        ones = sb("ones", [P, P])
        b_rows = sb("b_rows", [24, CW])
        cols = sb("cols", [P, 6, 44])
        silu_c = sb("silu_c", [P, KT])
        c_rows = sb("c_rows", [KT, P])
        b_cols = sb("b_cols", [P, QT, 24])
        mod_s = sb("mod_s", [P, KT])
        mod_b = sb("mod_b", [P, KT])
        sink_row = sb("sink_row", [P, HEADS])
        stat = sb("stat", [P, 11])

        with ExitStack() as att:
            def sba(name, shape, dt=F32):
                return att.enter_context(nc.sbuf_tensor(name, shape, dt))
            logit = sba("logit", [P, 2, 4, S])
            probT = sba("probT", [P, 2, 4 * P])
            v_tok = sba("v_tok", [P, NB, 4, HD])
            score = sba("score", [P, NB, S])
            w_tok = sba("w_tok", [P, NB, P])
            bias = sba("bias", [P, 4, S])
            dist = sba("dist", [P, 3 * P])
            mask_c = sba("mask_c", [P, 3 * P])
            mask_w = sba("mask_w", [P, 3 * P])
            mask_a = sba("mask_a", [P, 3 * P])
            top8 = sba("top8", [P, NB, 8])
            mx = sba("mx", [P, 2, 4])
            nmx = sba("nmx", [P, 2, 4])
            den = sba("den", [P, 2, 4])
            sink_e = sba("sink_e", [P, 2, 4])
            sink_d = sba("sink_d", [P, 2, 4])
            rden = sba("rden", [P, 2, 4])
            ki_dup = sba("ki_dup", [P, S])
        for n in range(2, PAIR):
            pair_hi[n] = sb(f"pair_hi{n}", [P, 2048], F32R)
            pair_lo[n] = sb(f"pair_lo{n}", [P, 2048], F32R)
        with ExitStack() as ffn:
            def sbf(name, shape, dt=F32):
                return ffn.enter_context(nc.sbuf_tensor(name, shape, dt))
            act_hi = sbf("act_hi", [P, CT, S], F32R)
            act_lo = sbf("act_lo", [P, CT, S], F32R)
            conv = sbf("conv", [P, CT, S])
            y = sbf("y", [P, NB, D])
        proj = sb("proj", [P, NT, S])

        ps = ctx.enter_context(nc.psum_tensor("ps", [P, 8, 512], F32))

        raw_in = [sem(f"raw_in{n}") for n in range(RAW)]
        pair_in = [sem(f"pair_in{n}") for n in range(RAW)]
        ada_sum = sem("ada_sum")
        w_split = sem("w_split")
        q_used = sem("q_used")
        w_hi = sem("w_hi")
        w_used = sem("w_used")
        x_in = [sem(f"x_in{b}") for b in range(NB)]
        c_in = sem("c_in")
        rows_in = sem("rows_in")
        sink_in = sem("sink_in")
        const_ready = sem("const_ready")
        masks_ready = sem("masks_ready")
        chosen = sem("chosen")
        alibi_done = sem("alibi_done")
        bias_ready = sem("bias_ready")
        c_act = sem("c_act")
        cols_ps = sem("cols_ps")
        cols_ready = sem("cols_ready")
        sq_done = sem("sq_done")
        var_done = sem("var_done")
        root_done = sem("root_done")
        rstd_done = sem("rstd_done")
        xn_ready = sem("xn_ready")
        xnT_ready = sem("xnT_ready")
        mod_ps = sem("mod_ps")
        mod_done = sem("mod_done")
        h_ready = sem("h_ready")
        h_hi = sem("h_hi")
        h_lo = sem("h_lo")
        ki_in = sem("ki_in")
        ki_hi_done = sem("ki_hi_done")
        ki_split = sem("ki_split")
        ki_used = sem("ki_used")
        win_added = sem("win_added")
        ki_added = sem("ki_added")
        proj_zero = sem("proj_zero")
        bank_zero = sem("bank_zero")
        gate_ps = sem("gate_ps")
        gate_done = sem("gate_done")
        q_scaled = sem("q_scaled")
        dup_in = sem("dup_in")
        vT_ps = sem("vT_ps")
        v_ready = sem("v_ready")
        idx_ps = sem("idx_ps")
        idx_relu = sem("idx_relu")
        topk_done = [sem(f"topk_done{b}") for b in range(NB)]
        idx_sum = sem("idx_sum")
        lg_ps = sem("lg_ps")
        lg_done = sem("lg_done")
        e_done = sem("e_done")
        p_ready = sem("p_ready")
        pT_ps = sem("pT_ps")
        pT_ready = sem("pT_ready")
        o_ps = sem("o_ps")
        o_hi = sem("o_hi")
        o_lo = sem("o_lo")
        mix_step = sem("mix_step")
        rows2_ps = sem("rows2_ps")
        rows2_done = sem("rows2_done")
        mod2_ps = sem("mod2_ps")
        mod2_done = sem("mod2_done")
        gate_zero = sem("gate_zero")
        gate_begun = sem("gate_begun")
        y_zero = sem("y_zero")
        conv_a = sem("conv_a")
        conv_step = sem("conv_step")
        silu_done = sem("silu_done")
        gu_done = sem("gu_done")
        act_hi_done = sem("act_hi_done")
        act_split = sem("act_split")
        y_added = sem("y_added")
        gate2_ps = sem("gate2_ps")
        gate2_done = sem("gate2_done")
        x_step = sem("x_step")
        gf_in = sem("gf_in")
        gained = sem("gained")
        y_out = sem("y_out")
        y_ready = sem("y_ready")
        out_done = sem("out_done")
        chain = sem("chain")

        C_GM, C_GF, C_W0, C_W1, C_W2, C_B = range(6)

        def unit_bias(u):
            if u % 3 == 2:
                return bias
            if u % 3 == 0:
                return h32
            return xn.rearrange("p b (a k) -> p (b a) k", k=S)

        def in_chunk(q, w):
            return w_in[0, bass.ds(q * CW, CW), WIN_COL[w]:WIN_COL[w] + CW]

        def quarter(ap):
            return ap.rearrange("(k p) n -> p k n", p=P)

        def used(seg, count):
            after = seg in (FFN_A, FFN, LAST) or seg is FFN_1 and count >= UP0.of_kind("W", 7)
            return PAIR + count + (2 if after else 0)

        UP_END = PAIR + UP0.of_kind("W", 7)

        def split(count):
            return count + RAW

        def sums(count, seg=None):
            if seg is None and GATE1_END < count <= SHIFT2_END:
                return PAIRED + GATE1_END + 2 * (count - GATE1_END)
            if seg is IN or seg is None and count <= PAIRED:
                return 2 * count
            if seg is None and count <= GATE1_END:
                return PAIRED + count
            return PAIRED + count + SHIFT2_END - GATE1_END

        PAIRED = IN3.before["A"]
        GATE1_END = PAIRED + KT
        SHIFT2_END = GATE1_END + KT

        block = ctx.enter_context(nc.Block())

        @block.sync
        def _(sp):
            segs = [ADA0, IN, IN3, MID, UP0, FFN_1, FFN_A, FFN, LAST]

            def load(seg, j, i, src, tiles=QT):
                waits = []
                if seg is not ADA0 or j >= RAW:
                    if j >= RAW:
                        need = {seg.kinds[j - RAW]: seg.of_kind(seg.kinds[j - RAW], j - RAW, i)}
                    else:
                        ends = [segs[segs.index(seg) - 1].kinds] + [seg.kinds] * (seg.times > 1)
                        need = {}
                        for kind in {end[j - RAW] for end in ends}:
                            after = min(end[len(end) + j - RAW + 1:].count(kind)
                                        for end in ends if end[j - RAW] == kind)
                            need[kind] = seg.before[kind] - after + i * seg.kinds.count(kind)
                    for kind, count in need.items():
                        what, count = {"A": (ada_sum, sums(count, seg if seg.times > 1 else None)),
                                       "W": (w_split, split(count)), "Q": (q_used, count)}[kind]
                        waits.append((what, sp.lower_val(count)))
                if len(waits) == 2:
                    sp.wait_ge(*waits[1])
                dst = raw[:, seg.slot(j), :].rearrange("p (k n) -> p k n", k=tiles)
                if isinstance(src, list):
                    dst = raw[:, seg.slot(j), :].rearrange("p (k v n) -> p k v n", k=2, v=2)
                    dma = sp.dma_start(dst[:, 0], src[0])
                    dma.then_inc(raw_in[seg.slot(j)], 16)
                    sp.dma_start(dst[:, 1], src[1]).then_inc(pair_in[seg.slot(j)], 16)
                else:
                    dma = sp.dma_start(dst, src)
                    dma.then_inc(raw_in[seg.slot(j)], 16)
                if waits:
                    dma.wait_op(*waits[0], "sem-ge")

            def ada_pair(q, n):
                return [w_ada[0, (2 * n + k) * P:(2 * n + k + 1) * P, SHIFT1 * D:(SCALE1 + 1) * D]
                        .rearrange("p (v c) -> p v c", v=2)[:, :, bass.ds(q * CW, CW)] for k in range(2)]

            def ada(which, k):
                return w_ada[0, bass.ds(k * P, P), which * D:(which + 1) * D].rearrange("p (k n) -> p k n", k=1)

            sp.dma_start(ki_raw[:, :, :], quarter(w_in[0, 0:CW, SMALL_COL:SMALL_COL + SMALL]))\
                .then_inc(ki_in, 16)
            for j in range(8):
                load(ADA0, j, 0, ada_pair(0, j))
            load(ADA0, 8, 0, quarter(in_chunk(0, 0)))
            in_load = {}
            with sp.Fori(0, 3) as q:
                for n, j in enumerate(IN.js("A")):
                    in_load[j] = ada_pair(q + 1, n)
                for n, j in enumerate(IN.js("W")):
                    in_load[j] = quarter(in_chunk(q, n + 1) if n < 7 else in_chunk(q + 1, 0))
                for j in range(len(IN.kinds)):
                    load(IN, j, q, in_load[j])
                sp.wait_ge(ki_split, q + 1)
                sp.wait_ge(ki_in, 16)
                sp.dma_start(ki_raw[:, :, :],
                             quarter(w_in[0, bass.ds((q + 1) * CW, CW), SMALL_COL:SMALL_COL + SMALL]))\
                    .then_inc(ki_in, 16)
            for n, j in enumerate(IN3.js("A")):
                in_load[j] = ada(GATE1, n)
            for n, j in enumerate(IN3.js("W")):
                in_load[j] = quarter(in_chunk(3, n + 1))
            for j in range(len(IN3.kinds)):
                load(IN3, j, 0, in_load[j], 1 if IN3.kinds[j] == "A" else QT)
            mid_a = iter([ada(GATE1, n) for n in range(8, KT)] + [
                w_ada[0, n * 2 * P:(n + 1) * 2 * P, SHIFT2 * D + h * 1024:SHIFT2 * D + (h + 1) * 1024]
                .rearrange("(k p) n -> p k n", p=P) for h in range(2) for n in range(8)])
            mid_q = iter([ada(SCALE2, n) for n in range(KT)])
            mid_w = iter([w_o[0, n * 2 * P:(n + 1) * 2 * P, h * 1024:(h + 1) * 1024]
                          .rearrange("(k p) n -> p k n", p=P) for h in range(2) for n in MIX_PAIRS])
            for j, kind in enumerate(MID.kinds):
                tiles = 2 if kind == "W" or j in MID.js("A")[8:] else 1
                load(MID, j, 0, next({"A": mid_a, "Q": mid_q, "W": mid_w}[kind]), tiles)

            def up(g, n):
                w = (w_gate, w_up)[n % 2]
                return quarter(w[0, (n // 2) * CW:(n // 2 + 1) * CW, bass.ds(g * CW, CW)])

            def down(g, n):
                return w_down[0, bass.ds(g * CW + (n % 2) * 2 * P, 2 * P),
                              (n // 2) * 1024:(n // 2 + 1) * 1024].rearrange("(k p) n -> p k n", p=P)

            def ffn_body(seg, i, g):
                ws = iter([(up(g, n), QT) for n in range(4)] + [(down(g - 1, n), 2) for n in range(2)]
                          + [(up(g, n), QT) for n in range(4, 8)] + [(down(g - 1, n), 2) for n in range(2, 4)])
                a = 0
                for j, kind in enumerate(seg.kinds):
                    if kind == "A":
                        load(seg, j, i, ada(GATE2, (g - 1) * QT + a), 1)
                        a += 1
                    else:
                        src, tiles = next(ws)
                        load(seg, j, i, src, tiles)

            for n in range(8):
                load(UP0, n, 0, up(0, n))
            ffn_body(FFN_1, 0, 1)
            with sp.Fori(0, FFN_A.times) as i:
                ffn_body(FFN_A, i, i + 2)
            with sp.Fori(0, FFN.times) as i:
                ffn_body(FFN, i, i + 2 + FFN_A.times)
            for n in range(4):
                load(LAST, n, 0, down(PASSES - 1, n), 2)
            sp.wait_ge(w_split, split(LAST.of_kind("W", 0)))
            sp.dma_start(raw[:, 0, :], g_final[None, :].to_broadcast([P, D])).then_inc(gf_in, 16)
            for b, h, done, count in ((0, 0, y_out, 1), (0, 1, y_out, 2), (1, 0, y_ready, 1), (1, 1, y_out, 3)):
                half = slice(h * 1024, (h + 1) * 1024)
                sp.wait_ge(done, count)
                sp.dma_start(out[0, b * P:(b + 1) * P, half], raw[:, 2 + b, half]).then_inc(out_done, 16)
            sp.wait_ge(out_done, 16 * NB * 2)

        @block.gpsimd
        def _(pool):
            nc.gpsimd.memset(ident[:, :], 0.0).then_inc(const_ready, 1)
            pool.wait_ge(const_ready, 1)
            nc.gpsimd.affine_select(out=ident[:, :], in_=ident[:, :], compare_op=ALU.not_equal, fill=1.0,
                                    base=0, pattern=[[-1, P]], channel_multiplier=1).then_inc(const_ready, 1)
            nc.gpsimd.memset(rows[:, :, :], 0.0).then_inc(const_ready, 1)
            nc.gpsimd.memset(ones[:, :], 1.0).then_inc(const_ready, 1)
            nc.gpsimd.memset(proj[:, :, :], 0.0).then_inc(proj_zero, 1)
            pool.wait_ge(cols_ps, 2)
            nc.gpsimd.memset(gate_row[:, :], 0.0).then_inc(gate_zero, 1)
            pool.wait_ge(gate_zero, 1)
            pool.dma_start(gate_row[0:1, :], b_ada[0:1, GATE1 * D:(GATE1 + 1) * D]).then_inc(gate_begun, 16)
            pool.wait_ge(w_used, used(IN3, NQ * NWIN))
            nc.gpsimd.iota(dist[:, 0:P], pattern=[[-1, P]], base=0, channel_multiplier=1,
                           allow_small_or_imprecise_dtypes=True)
            nc.gpsimd.iota(dist[:, P:3 * P], pattern=[[-1, S]], base=P, channel_multiplier=1,
                           allow_small_or_imprecise_dtypes=True).then_inc(masks_ready, 1)
            nc.gpsimd.memset(mask_c[:, :], 0.0).then_inc(masks_ready, 1)
            pool.wait_ge(masks_ready, 2)
            nc.gpsimd.affine_select(out=mask_c[:, 0:P], in_=mask_c[:, 0:P], compare_op=ALU.is_ge, fill=NEG,
                                    base=0, pattern=[[-1, P]], channel_multiplier=1).then_inc(masks_ready, 1)
            nc.gpsimd.affine_select(out=mask_c[:, P:3 * P], in_=mask_c[:, P:3 * P], compare_op=ALU.is_ge,
                                    fill=NEG, base=P, pattern=[[-1, S]], channel_multiplier=1)\
                .then_inc(masks_ready, 1)
            pool.wait_ge(masks_ready, 4)
            nc.gpsimd.tensor_copy(mask_w[:, 0:P], mask_c[:, 0:P]).then_inc(masks_ready, 1)
            nc.gpsimd.affine_select(out=mask_w[:, P:3 * P], in_=mask_c[:, P:3 * P], compare_op=ALU.is_ge,
                                    fill=NEG, base=WINDOW - 1 - P, pattern=[[1, S]], channel_multiplier=-1)\
                .then_inc(masks_ready, 1)
            pool.wait_ge(masks_ready, 6)
            for u in range(8):
                g, b = divmod(u, NB)
                w = P * (b + 1)
                m = slice(b * P, b * P + w)
                if g >= KV:
                    pool.wait_ge(chosen, b + 1)
                if u >= 3:
                    pool.wait_ge(lg_done, u - 2)
                for r in range(4):
                    slope = SLOPE[2 * (4 * (g % KV) + r) + (1 if g < KV else 0)]
                    nc.gpsimd.tensor_scalar(unit_bias(u)[:, r, 0:w], dist[:, m], -slope, None, ALU.mult)\
                        .then_inc(alibi_done, 1)
                pool.wait_ge(alibi_done, 4 * (u + 1))
                for r in range(4):
                    ins = nc.gpsimd.tensor_tensor(unit_bias(u)[:, r, 0:w], unit_bias(u)[:, r, 0:w],
                                                  (mask_w if g < KV else mask_a)[:, m], ALU.add)
                ins.then_inc(bias_ready, 1)
            pool.wait_ge(rows2_ps, 1)
            nc.gpsimd.memset(y[:, :, :], 0.0).then_inc(y_zero, 1)
            pool.wait_ge(mix_step, 8)
            nc.gpsimd.memset(gate_row[:, :], 0.0).then_inc(gate_zero, 1)
            pool.wait_ge(gate_zero, 2)
            pool.dma_start(gate_row[0:1, :], b_ada[0:1, GATE2 * D:(GATE2 + 1) * D]).then_inc(gate_begun, 16)

        @block.scalar
        def _(act):
            def split_hi(seg, j, i=0):
                m = seg.of_kind("W", j, i)
                act.wait_ge(raw_in[seg.slot(j)], 16 * seg.loads(j, i))
                act.wait_ge(w_used, used(seg, m - PAIR))
                nc.scalar.copy(pair_hi[seg.pair(j)][:, :], raw[:, seg.slot(j), :]).then_inc(w_hi, 1)

            def split_ki(q):
                act.wait_ge(ki_in, 16 * (q + 1))
                nc.scalar.copy(ki_hi[:, :, :], ki_raw[:, :, :]).then_inc(ki_hi_done, 1)

            def squares(n, b, h, banks):
                if n == 0 and (b or h):
                    act.wait_ge(sq_done, 2 * b + h)
                nc.scalar.activation(ps[:, banks:banks + 2, :].rearrange("p a n -> p (a n)"),
                                     x_sb[:, b, h * 1024:(h + 1) * 1024], ACT.Square,
                                     accum_out=stat[:, 2 * h + b:2 * h + b + 1]).then_inc(sq_done, 1)

            def load_root():
                nc.scalar.activation(stat[:, 10:11], ones[:, 0:1], ACT.Sqrt)

            def root(n):
                act.wait_ge(var_done, 2 * (n + 1))
                nc.scalar.activation(stat[:, 6:8], stat[:, 4:6], ACT.Sqrt).then_inc(root_done, 1)

            def normalise(q, n, norm):
                act.wait_ge(rstd_done, norm + 1)
                if later(n):
                    act.wait_ge(xnT_ready, n)
                for b in range(NB):
                    ins = nc.scalar.activation(xn[:, b, :], x_sb[:, b, bass.ds(q * CW, CW)], ACT.Copy,
                                               scale=stat[:, 8 + b:9 + b])
                ins.then_inc(xn_ready, 1)

            def modulated(q, n, tile):
                bank = 0 if isinstance(n, int) and n >= NQ else 5
                act.wait_ge(xnT_ready, n + 1)
                if isinstance(n, int) and n >= NQ:
                    act.wait_ge(mod2_done, 2)
                else:
                    act.wait_ge(mod_done, 3 * n + 3)
                if later(n):
                    act.wait_ge(h_lo, n)
                for t in range(QT):
                    ins = nc.scalar.activation(h32[:, t, :], ps[:, bank + t // 2, (t % 2) * S:(t % 2) * S + S],
                                               ACT.Identity, bias=mod_b[:, bass.ds(q * QT + t, 1)],
                                               scale=mod_s[:, bass.ds(q * QT + t, 1)])
                ins.then_inc(h_ready, 1)
                act.wait_ge(h_ready, n + 1)
                nc.scalar.copy(op_hi[:, bass.ds(tile, QT), :], h32[:, :, :]).then_inc(h_hi, 1)

            act.dma_start(c_rows[:, :], c[0, :].rearrange("(k p) -> k p", p=P)).then_inc(c_in, 16)
            for b in range(NB):
                act.dma_start(x_sb[:, b, :], x[0, b * P:(b + 1) * P, :]).then_inc(x_in[b], 16)
            act.wait_ge(c_in, 16)
            nc.scalar.activation(c_rows[:, :], c_rows[:, :], ACT.Silu).then_inc(c_act, 1)
            act.dma_start(b_rows[:, :], b_ada[0, :].rearrange("(k p) -> k p", p=CW)).then_inc(rows_in, 16)
            act.wait_ge(const_ready, 3)
            act.dma_start(rows[0:KT, C_GM, :], g_mix[0, :].rearrange("(k p) -> k p", p=P)).then_inc(rows_in, 16)
            act.dma_start(rows[0:KT, C_GF, :], g_ffn[0, :].rearrange("(k p) -> k p", p=P)).then_inc(rows_in, 16)
            for n in range(3):
                act.dma_start(rows[0:FT, C_W0 + n, :], conv_w[0, n, :].rearrange("(k p) -> k p", p=P))\
                    .then_inc(rows_in, 16)
            act.dma_start(rows[0:FT, C_B, :], conv_b[0, :].rearrange("(k p) -> k p", p=P)).then_inc(rows_in, 16)
            act.dma_start(sink_row[:, :], sinks[0:1, :].to_broadcast([P, HEADS])).then_inc(sink_in, 16)
            for b in range(NB):
                act.wait_ge(x_in[b], 16)
                for h in range(2):
                    squares(0, b, h, 4)
            root(0)
            normalise(0, 0, 0)
            split_hi(ADA0, 8)
            modulated(0, 0, 0)

            def in_phase(seg, i, q):
                for w, j in enumerate(seg.js("W"), 1):
                    split_hi(seg, j, i)
                    if w == 1:
                        split_ki(q)
                    if w == 2 and seg is IN:
                        normalise(q + 1, q + 1, 0)
                if seg is IN:
                    modulated(q + 1, q + 1, (q + 1) * QT)

            with act.Fori(0, 3) as q:
                in_phase(IN, q, q)
            in_phase(IN3, 0, 3)

            act.wait_ge(ki_added, NQ)
            act.wait_ge(win_added, NQ * NWIN + 2)
            act.dma_start(ki_dup[IDXD:2 * IDXD, :], proj[0:IDXD, T_KI, :]).then_inc(dup_in, 16)
            for t in (T_QB, T_QA):
                nc.scalar.mul(proj[:, t:t + HEADS, :], proj[:, t:t + HEADS, :], HD ** -0.5)\
                    .then_inc(q_scaled, 1)
            for n in range(8):
                act.wait_ge(idx_ps, n + 1)
                if n >= 2:
                    act.wait_ge(idx_sum, 4 * (n - 1))
                w = P * (n // 4 + 1)
                s = n % 2
                nc.scalar.activation(logit[:, s, :, 0:w],
                                     ps[:, 2 * s:2 * s + 2, :].rearrange("p a (h k) -> p (a h) k", h=2)[:, :, 0:w],
                                     ACT.Relu).then_inc(idx_relu, 1)
            def exps(u):
                g, b = divmod(u, NB)
                w = P * (b + 1)
                act.wait_ge(lg_done, u + 1)
                for r in range(4):
                    ins = nc.scalar.activation(logit[:, u % 2, r, 0:w], logit[:, u % 2, r, 0:w], ACT.Exp,
                                               bias=nmx[:, u % 2, r:r + 1], accum_out=den[:, u % 2, r:r + 1])
                if g < KV:
                    ins = nc.scalar.activation(sink_e[:, u % 2, :], sink_d[:, u % 2, :], ACT.Exp)
                ins.then_inc(e_done, 1)

            def transposed(u):
                act.wait_ge(pT_ps, u + 1)
                if u:
                    act.wait_ge(o_ps, u)
                b = u % NB
                nc.scalar.copy(probT[:, 0:b + 1, :], ps[:, 4:5 + b, :]).then_inc(pT_ready, 1)

            def output(u):
                g, b = divmod(u, NB)
                act.wait_ge(o_ps, u + 1)
                t = (HEADS if g < KV else 0) + 4 * (g % KV)
                nc.scalar.copy(op_hi[:, t:t + 4, b * P:(b + 1) * P],
                               ps[:, 6, :].rearrange("p (h q) -> p h q", h=4)).then_inc(o_hi, 1)

            exps(0)
            exps(1)
            for u in range(8):
                if u:
                    output(u - 1)
                transposed(u)
                if u + 2 < 8:
                    exps(u + 2)
                else:
                    split_hi(MID, MID.js("W")[u - 6])
            output(7)
            for n, j in enumerate(MID.js("W")):
                if n >= 2:
                    split_hi(MID, j)
                if n >= 4 and n < 8:
                    act.wait_ge(gate_ps, n - 3)
                    nc.scalar.copy(gate_row[:, (n - 4) * CW:(n - 3) * CW], ps[:, GATE_BANK[n - 4], :])\
                        .then_inc(gate_done, 1)
                if n == 12:
                    load_root()
                if n in (13, 14):
                    b = n - 13
                    act.wait_ge(mix_step, 2 * b + 2)
                    squares(1, b, 0, 2 * b)
            for n in range(UP_AHEAD):
                split_hi(UP0, n)
            for b in range(NB):
                act.wait_ge(mix_step, 6 + 2 * b)
                squares(1, b, 1, 4 + 2 * b)
            root(1)

            normalise(0, NQ, 1)
            for q in range(NQ):
                if q < NQ - 1:
                    normalise(q + 1, NQ + q + 1, 1)
                modulated(q, NQ + q, QT * q)
                split_hi(UP0, UP_AHEAD + q)
            split_hi(UP0, 7)

            def conv_tail(g):
                base = 4 if isinstance(g, int) and g == 0 else 0
                for n, t in enumerate(TILE_ORDER):
                    if n == 0:
                        act.wait_ge(w_used, UP_END + 12 * g)
                    if n >= 2:
                        act.wait_ge(conv_step, 2 * CT * g + 2 * (n - 1))
                    nc.scalar.activation(conv[:, t, :], ps[:, base + t // 2, (t % 2) * S:(t % 2) * S + S], ACT.Identity,
                                         bias=cols[:, C_B, bass.ds(g * CT + t, 1)],
                                         scale=cols[:, C_W2, bass.ds(g * CT + t, 1)]).then_inc(conv_a, 1)
                act.wait_ge(conv_step, 2 * CT * (g + 1))
                nc.scalar.activation(conv[:, :, :], conv[:, :, :], ACT.Silu).then_inc(silu_done, 1)
                act.wait_ge(gu_done, g + 1)
                act.wait_ge(w_used, UP_END + 2 + 12 * g)
                nc.scalar.copy(act_hi[:, :, :], conv[:, :, :]).then_inc(act_hi_done, 1)

            def ffn_body(seg, i, g):
                for n, j in enumerate(seg.js("W")):
                    split_hi(seg, j, i)
                    if n == (2 if seg is FFN_1 else 1):
                        conv_tail(g - 1)

            ffn_body(FFN_1, 0, 1)
            with act.Fori(0, FFN_A.times) as i:
                ffn_body(FFN_A, i, i + 2)
            with act.Fori(0, FFN.times) as i:
                ffn_body(FFN, i, i + 2 + FFN_A.times)
            split_hi(LAST, 0)
            split_hi(LAST, 1)
            conv_tail(PASSES - 1)
            act.wait_ge(gate2_ps, 1)
            nc.scalar.copy(gate_row[:, :], ps[:, 0:4, :].rearrange("p a n -> p (a n)")).then_inc(gate2_done, 1)
            split_hi(LAST, 2)
            split_hi(LAST, 3)
            load_root()
            for b in range(NB):
                act.wait_ge(x_step, 6 + 2 * b)
                squares(2, b, 0, 4 + 2 * b)
            for b in range(NB):
                act.wait_ge(x_step, 10 + 2 * b)
                squares(2, b, 1, 2 * b)
                act.wait_ge(var_done, 6 + 2 * b)
                nc.scalar.activation(stat[:, 6 + b:7 + b], stat[:, 4 + b:5 + b], ACT.Sqrt).then_inc(root_done, 1)
                act.wait_ge(rstd_done, 3 + b)
                act.wait_ge(gained, 3 + b)
                for h in range(b, 2):
                    half = raw[:, 2 + b, h * 1024:(h + 1) * 1024]
                    nc.scalar.activation(half, half, ACT.Copy, scale=stat[:, 8 + b:9 + b]).then_inc(y_out, 1)

        @block.vector
        def _(dve):
            chained = [0]

            def link(ins):
                chained[0] += 1
                ins.then_inc(chain, 1)
                dve.wait_ge(chain, chained[0])

            def split_lo(seg, j, i=0):
                dve.wait_ge(w_hi, seg.of_kind("W", j, i))
                nc.vector.tensor_tensor(pair_lo[seg.pair(j)][:, :], raw[:, seg.slot(j), :],
                                        pair_hi[seg.pair(j)][:, :].bitcast(F32), ALU.subtract).then_inc(w_split, 1)

            def add_ada(seg, j, i, acc, k, pairs=False):
                n = seg.of_kind("A", j, i)
                dve.wait_ge(raw_in[seg.slot(j)], 16 * seg.loads(j, i))
                for t in range(2 if pairs else 1):
                    tile = 2 * k + t if pairs else k
                    w = raw[:, seg.slot(j), t * 1024:(t + 1) * 1024] if pairs else raw[:, seg.slot(j), :]
                    if t and seg is not MID:
                        dve.wait_ge(pair_in[seg.slot(j)], 16 * paired_loads(seg, j, i))
                    col = silu_c[:, bass.ds(tile, 1)]
                    if seg in (IN3, FFN_1) and tile == 0:
                        dve.wait_ge(gate_begun, 16 if seg is IN3 else 32)
                        ins = nc.vector.scalar_tensor_tensor(acc, w, col, acc, ALU.mult, ALU.add)
                    elif isinstance(tile, int) and tile == 0:
                        ins = nc.vector.tensor_scalar(acc, w, col, None, ALU.mult)
                    else:
                        dve.wait_ge(ada_sum, sums(n - 1, seg if seg.times > 1 else None) + t)
                        ins = nc.vector.scalar_tensor_tensor(acc, w, col, acc, ALU.mult, ALU.add)
                    ins.then_inc(ada_sum, 1)

            def paired_loads(seg, j, i):
                if seg is ADA0:
                    return j // RAW + 1
                own = [a for a in seg.js("A") if a % RAW == j % RAW]
                return 2 + own.index(j) + 1 + i * len(own)

            nc.vector.memset(ps[:, 2:4, :], 0.0).then_inc(bank_zero, 1)
            dve.wait_ge(cols_ps, 1)
            nc.vector.tensor_copy(silu_c[:, :], ps[:, 7, 0:KT]).then_inc(cols_ready, 1)
            dve.sem_inc(w_split, RAW)
            dve.wait_ge(cols_ready, 1)

            def rms(n):
                dve.wait_ge(sq_done, 2 * NB * (n + 1))
                nc.vector.tensor_tensor(stat[:, 4:6], stat[:, 0:2], stat[:, 2:4], ALU.add).then_inc(var_done, 1)
                dve.wait_ge(var_done, 2 * n + 1)
                nc.vector.tensor_scalar(stat[:, 4:6], stat[:, 4:6], 1.0 / D, EPS, ALU.mult, ALU.add)\
                    .then_inc(var_done, 1)
                dve.wait_ge(root_done, n + 1)
                nc.vector.reciprocal(stat[:, 8:10], stat[:, 6:8]).then_inc(rstd_done, 1)

            def mod_columns(q, n):
                dve.wait_ge(mod_ps, n + 1)
                sc, sh = (b_cols[:, :, bass.ds(v * NQ + q, 1)].rearrange("p t a -> p (t a)")
                          for v in (SCALE1, SHIFT1))
                to_s, to_b = (m[:, bass.ds(q * QT, QT)] for m in (mod_s, mod_b))
                nc.vector.tensor_tensor(to_s, ps[:, 7, QT:2 * QT], sc, ALU.add).then_inc(mod_done, 1)
                nc.vector.tensor_tensor(to_b, ps[:, 7, 0:QT], sh, ALU.add).then_inc(mod_done, 1)
                dve.wait_ge(mod_done, 3 * n + 2)
                nc.vector.scalar_tensor_tensor(to_s, to_s, 1.0, cols[:, C_GM, bass.ds(q * QT, QT)],
                                               ALU.add, ALU.mult).then_inc(mod_done, 1)
                dve.wait_ge(mod_done, 3 * n + 3)

            def h_low(n, tile):
                dve.wait_ge(h_hi, n + 1)
                nc.vector.tensor_tensor(op_lo[:, bass.ds(tile, QT), :], h32[:, :, :],
                                        op_hi[:, bass.ds(tile, QT), :].bitcast(F32), ALU.subtract).then_inc(h_lo, 1)

            for j in range(8):
                add_ada(ADA0, j, 0, ada_acc[:, :, :].rearrange("p v n -> p (v n)"), j, True)
                if j == 5:
                    dve.wait_ge(cols_ps, 2)
                    nc.vector.tensor_copy(cols[:, :, :], ps[:, 6, 0:6 * 44].rearrange("p (a n) -> p a n", a=6))\
                        .then_inc(cols_ready, 1)
                    nc.vector.tensor_copy(b_cols[:, :, :], ps[:, 6, 6 * 44:6 * 44 + QT * 24]
                                          .rearrange("p (t n) -> p t n", t=QT)).then_inc(cols_ready, 1)
                if j == 4:
                    rms(0)
            split_lo(ADA0, 8)
            dve.sem_inc(win_added, 1)
            dve.wait_ge(cols_ready, 3)
            mod_columns(0, 0)
            h_low(0, 0)
            dve.wait_ge(proj_zero, 1)
            dve.wait_ge(bank_zero, 1)

            def add_window(v, w):
                dve.wait_ge(w_used, used(IN, v))
                b = 2 * (w % 2)
                dst = proj[:, WIN_TILE[w]:WIN_TILE[w] + CT, :]
                nc.vector.tensor_tensor(dst, dst, ps[:, b:b + 2, :].rearrange("p a (t n) -> p (a t) n", t=2),
                                        ALU.add).then_inc(win_added, 1)

            def in_phase(seg, i, q):
                a, w = 0, 1
                for j, kind in enumerate(seg.kinds):
                    if kind == "A":
                        if seg is IN:
                            add_ada(seg, j, i, ada_acc[:, :, :].rearrange("p v n -> p (v n)"), a, True)
                        else:
                            add_ada(seg, j, i, gate_row[:, :], a)
                        a += 1
                        continue
                    split_lo(seg, j, i)
                    if w == NWIN:
                        continue
                    if w == 1:
                        dve.wait_ge(ki_hi_done, q + 1)
                        nc.vector.tensor_tensor(ki_lo[:, :, :], ki_raw[:, :, :], ki_hi[:, :, :].bitcast(F32),
                                                ALU.subtract).then_inc(ki_split, 1)
                    add_window(q * NWIN + w - 1, (w - 2) % NWIN)
                    if w == 5:
                        dve.wait_ge(ki_used, q + 1)
                        nc.vector.tensor_tensor(proj[0:SMALL, T_KI, :], proj[0:SMALL, T_KI, :],
                                                ps[0:SMALL, 4, 0:S], ALU.add).then_inc(ki_added, 1)
                    w += 1
                if seg is IN:
                    mod_columns(q + 1, q + 1)
                    add_window(q * NWIN + NWIN - 1, 6)
                    h_low(q + 1, (q + 1) * QT)

            with dve.Fori(0, 3) as q:
                in_phase(IN, q, q)
            in_phase(IN3, 0, 3)
            for w in (6, 7):
                add_window(3 * NWIN + w + 1, w)

            dve.wait_ge(masks_ready, 1)
            for n in range(NB):
                dve.wait_ge(vT_ps, 1)
                ins = nc.vector.tensor_copy(v_tok[:, n, :, :], ps[:, 4 + n, :].rearrange("p (a d) -> p a d", a=4))
            ins.then_inc(v_ready, 1)
            nc.vector.tensor_scalar(w_tok[:, :, :], ps[:, 6, 0:2 * P].rearrange("p (b n) -> p b n", b=NB),
                                    (IDXD ** -0.5) * (IDXH ** -0.5), None, ALU.mult).then_inc(v_ready, 1)
            dve.wait_ge(v_ready, 2)

            mid_a = MID.js("A")
            shift_sum = [ada_acc[:, :, :].rearrange("p v n -> p (v n)"), y[:, 1, 0:1024]]

            def add_mid(a):
                if a < 8:
                    add_ada(MID, mid_a[a], 0, gate_row[:, :], 8 + a)
                else:
                    add_ada(MID, mid_a[a], 0, shift_sum[a // 8 - 1], a % 8, True)

            for n in range(8):
                blk, hh = divmod(n, 4)
                w = P * (blk + 1)
                dve.wait_ge(idx_relu, n + 1)
                for r in range(4):
                    head = 4 * hh + (0, 2, 1, 3)[r]
                    wcol = w_tok[:, blk, IDXD + head:IDXD + head + 1]
                    if hh == 0 and r == 0:
                        ins = nc.vector.tensor_scalar(score[:, blk, 0:w], logit[:, n % 2, r, 0:w], wcol, None,
                                                      ALU.mult)
                    else:
                        ins = nc.vector.scalar_tensor_tensor(score[:, blk, 0:w], logit[:, n % 2, r, 0:w], wcol,
                                                             score[:, blk, 0:w], ALU.mult, ALU.add)
                    ins.then_inc(idx_sum, 1)
                    dve.wait_ge(idx_sum, 4 * n + r + 1)
                if "A" in INDEX_KINDS[n]:
                    add_mid(n)

            dve.wait_ge(masks_ready, 6)
            steps = [0, 0]

            def topk_step(blk, ins):
                ins.then_inc(topk_done[blk], 1)
                steps[blk] += 1

            def topk_wait(blk):
                dve.wait_ge(topk_done[blk], steps[blk])

            part = [slice(0, P), slice(P, 3 * P)]
            for blk in range(NB):
                row = score[:, blk, 0:P * (blk + 1)]
                topk_step(blk, nc.vector.tensor_tensor(row, row, mask_c[:, part[blk]], ALU.add))
            for _ in range(TOPK // 8):
                for blk in range(NB):
                    topk_wait(blk)
                    topk_step(blk, nc.vector.max(top8[:, blk, :], score[:, blk, 0:P * (blk + 1)]))
                for blk in range(NB):
                    topk_wait(blk)
                    row = score[:, blk, 0:P * (blk + 1)]
                    topk_step(blk, nc.vector.match_replace(row, top8[:, blk, :], row, TAKEN))
            for blk in range(NB):
                topk_wait(blk)
                topk_step(blk, nc.vector.tensor_scalar(mask_a[:, part[blk]], score[:, blk, 0:P * (blk + 1)],
                                                       TAKEN / 2, NEG, ALU.is_gt, ALU.mult))
            for blk in range(NB):
                topk_wait(blk)
                nc.vector.tensor_tensor(mask_a[:, part[blk]], mask_a[:, part[blk]], mask_c[:, part[blk]],
                                        ALU.min).then_inc(chosen, 1)

            dve.wait_ge(sink_in, 16)

            def front(u):
                g, b = divmod(u, NB)
                w = P * (b + 1)
                dve.wait_ge(lg_ps, u + 1)
                dve.wait_ge(bias_ready, u + 1)
                if u >= 2:
                    dve.wait_ge(pT_ps, u - 1)
                for r in range(4):
                    head = 4 * (g % KV) + r
                    least = sink_row[:, head:head + 1] if g < KV else -3e38
                    ins = nc.vector.tensor_tensor_reduce(logit[:, u % 2, r, 0:w],
                                                   ps[:, 2 * (u % 2) + r // 2, (r % 2) * S:(r % 2) * S + w],
                                                   unit_bias(u)[:, r, 0:w], 1.0, least, ALU.add, ALU.max,
                                                   mx[:, u % 2, r:r + 1])
                link(ins)
                ins = nc.vector.tensor_scalar(nmx[:, u % 2, :], mx[:, u % 2, :], -1.0, None, ALU.mult)
                if g < KV:
                    ins = nc.vector.tensor_tensor(sink_d[:, u % 2, :], sink_row[:, 4 * g:4 * g + 4],
                                                  mx[:, u % 2, :], ALU.subtract)
                ins.then_inc(lg_done, 1)

            def back(u):
                g, b = divmod(u, NB)
                w = P * (b + 1)
                dve.wait_ge(e_done, u + 1)
                if g < KV:
                    link(nc.vector.tensor_tensor(den[:, u % 2, :], den[:, u % 2, :], sink_e[:, u % 2, :], ALU.add))
                link(nc.vector.reciprocal(rden[:, u % 2, :], den[:, u % 2, :]))
                for r in range(4):
                    ins = nc.vector.tensor_scalar(logit[:, u % 2, r, 0:w], logit[:, u % 2, r, 0:w],
                                                  rden[:, u % 2, r:r + 1], None, ALU.mult)
                ins.then_inc(p_ready, 1)

            def tail(u):
                g, b = divmod(u, NB)
                t = (HEADS if g < KV else 0) + 4 * (g % KV)
                dve.wait_ge(o_hi, u + 1)
                nc.vector.tensor_tensor(op_lo[:, t:t + 4, b * P:(b + 1) * P],
                                        ps[:, 6, :].rearrange("p (h q) -> p h q", h=4),
                                        op_hi[:, t:t + 4, b * P:(b + 1) * P].bitcast(F32), ALU.subtract)\
                    .then_inc(o_lo, 1)

            front(0)
            front(1)
            a, mid_w = sum(kinds.count("A") for kinds in INDEX_KINDS), iter(MID.js("W"))
            for u in range(8):
                back(u)
                if u:
                    tail(u - 1)
                for kind in UNIT_KINDS[u]:
                    if kind == "A":
                        add_mid(a)
                        a += 1
                    if kind == "W":
                        split_lo(MID, next(mid_w))
                if u + 2 < 8:
                    front(u + 2)
            tail(7)

            def add_mix(h, blocks):
                dve.wait_ge(w_used, used(MID, MID.of_kind("W", MID.js("W")[8 * h + 7])))
                if h == 0:
                    dve.wait_ge(gate_done, NQ)
                for b in blocks:
                    bank = 4 * h + 2 * b
                    step = 4 * h + 2 * b
                    mixed = ps[:, bank:bank + 2, :].rearrange("p a n -> p (a n)")
                    tmp = h32[:, :, :].rearrange("p a n -> p (a n)")
                    nc.vector.tensor_tensor(tmp, mixed, gate_row[:, h * 1024:(h + 1) * 1024], ALU.mult)\
                        .then_inc(mix_step, 1)
                    dve.wait_ge(mix_step, step + 1)
                    dst = x_sb[:, b, h * 1024:(h + 1) * 1024]
                    nc.vector.tensor_tensor(dst, dst, tmp, ALU.add).then_inc(mix_step, 1)
                    dve.wait_ge(mix_step, step + 2)

            def mod2(vec, bank):
                n = 0 if vec == SCALE2 else 1
                if n == 0:
                    dve.wait_ge(q_used, KT)
                else:
                    dve.wait_ge(rows2_ps, 1)
                nc.vector.tensor_copy(xn[:, n, :], ps[:, bank, :]).then_inc(rows2_done, 1)

            def mod2_columns(vec, bank, dst):
                n = 0 if vec == SCALE2 else 1
                dve.wait_ge(mod2_ps, n + 1)
                to = dst[:, :].rearrange("p (j t) -> p t j", j=NQ)
                nc.vector.tensor_tensor(to, ps[:, bank, :].rearrange("p (t j x) -> p t j x", t=QT, j=NQ)[:, :, :, 0],
                                        b_cols[:, :, vec * NQ:vec * NQ + NQ], ALU.add).then_inc(mod2_done, 1)
                dve.wait_ge(mod2_done, n + 1)

            w = 2
            for j in range(MID.js("W")[1] + 1, len(MID.kinds)):
                if MID.kinds[j] == "A":
                    add_mid(a)
                    a += 1
                    continue
                split_lo(MID, j)
                if w == 3:
                    mod2(SCALE2, 7)
                if w == 6:
                    mod2_columns(SCALE2, 4, mod_s)
                    link(nc.vector.scalar_tensor_tensor(mod_s[:, :], mod_s[:, :], 1.0, cols[:, C_GF, 0:KT],
                                                        ALU.add, ALU.mult))
                if w in (11, 12):
                    add_mix(0, [w - 11])
                w += 1
            for n in range(UP_AHEAD):
                split_lo(UP0, n)
                if n == 1:
                    mod2(SHIFT2, 0)
            add_mix(1, range(NB))
            mod2_columns(SHIFT2, 1, mod_b)
            rms(1)
            for q in range(NQ):
                h_low(NQ + q, QT * q)
                split_lo(UP0, UP_AHEAD + q)
            split_lo(UP0, 7)

            def conv_taps(g):
                base = 4 if isinstance(g, int) and g == 0 else 0
                for n, t in enumerate(TILE_ORDER):
                    dve.wait_ge(conv_a, g * CT + n + 1)
                    for lag, tap in ((1, C_W1), (2, C_W0)):
                        gate_ps_t = ps[:, base + t // 2, (t % 2) * S:(t % 2) * S + S - lag]
                        ins = nc.vector.scalar_tensor_tensor(conv[:, t, lag:S], gate_ps_t,
                                                             cols[:, tap, bass.ds(g * CT + t, 1)],
                                                             conv[:, t, lag:S], ALU.mult, ALU.add)
                        ins.then_inc(conv_step, 1)
                        dve.wait_ge(conv_step, g * 2 * CT + 2 * n + lag)
                dve.wait_ge(silu_done, g + 1)
                nc.vector.tensor_tensor(conv[:, :, :], conv[:, :, :],
                                        ps[:, base + 2:base + 4, :].rearrange("p a (t n) -> p (a t) n", t=2),
                                        ALU.mult).then_inc(gu_done, 1)
                dve.wait_ge(act_hi_done, g + 1)
                dve.wait_ge(gu_done, g + 1)
                nc.vector.tensor_tensor(act_lo[:, :, :], conv[:, :, :], act_hi[:, :, :].bitcast(F32),
                                        ALU.subtract).then_inc(act_split, 1)

            def add_y(h, count):
                dve.wait_ge(w_used, count)
                dst = y[:, :, h * 1024:(h + 1) * 1024]
                nc.vector.tensor_tensor(dst, dst, ps[:, 4:8, :].rearrange("p (b a) n -> p b (a n)", b=NB),
                                        ALU.add).then_inc(y_added, 1)

            def ffn_body(seg, i, g):
                a = 0
                w_js = seg.js("W")
                w = 0
                for j, kind in enumerate(seg.kinds):
                    if kind == "A":
                        add_ada(seg, j, i, gate_row[:, :], (g - 1) * QT + a)
                        a += 1
                        continue
                    split_lo(seg, j, i)
                    if w == (2 if seg is FFN_1 else 1):
                        conv_taps(g - 1)
                    if w == 3 and seg is not FFN_1:
                        add_y(1, used(seg, seg.of_kind("W", w_js[0], i) - 1))
                    if w == 8:
                        add_y(0, used(seg, seg.of_kind("W", w_js[5], i)))
                    w += 1

            dve.wait_ge(y_zero, 1)
            ffn_body(FFN_1, 0, 1)
            with dve.Fori(0, FFN_A.times) as i:
                ffn_body(FFN_A, i, i + 2)
            with dve.Fori(0, FFN.times) as i:
                ffn_body(FFN, i, i + 2 + FFN_A.times)
            split_lo(LAST, 0)
            split_lo(LAST, 1)
            conv_taps(PASSES - 1)
            add_y(1, used(LAST, LAST.of_kind("W", 0) - 1))
            split_lo(LAST, 2)
            split_lo(LAST, 3)

            steps = [0]

            def step(ins):
                steps[0] += 1
                ins.then_inc(x_step, 1)
                dve.wait_ge(x_step, steps[0])

            def scaled(b, half):
                step(nc.vector.tensor_tensor(y[:, b, half], y[:, b, half], gate_row[:, half], ALU.mult))
                step(nc.vector.tensor_tensor(x_sb[:, b, half], x_sb[:, b, half], y[:, b, half], ALU.add))

            def last_gain(b, half):
                nc.vector.tensor_tensor(raw[:, 2 + b, half], x_sb[:, b, half], raw[:, 0, half], ALU.mult)\
                    .then_inc(gained, 1)

            halves = slice(0, 1024), slice(1024, 2048)
            dve.wait_ge(gate2_done, 1)
            dve.wait_ge(y_added, 2 * PASSES - 2)
            for b in range(NB):
                scaled(b, halves[1])
            add_y(0, used(LAST, LAST.of_kind("W", 1)))
            dve.wait_ge(y_added, 2 * PASSES - 1)
            for b in range(NB):
                scaled(b, halves[0])
            dve.wait_ge(gf_in, 16)
            for b in range(NB):
                last_gain(b, halves[0])
            dve.wait_ge(w_used, used(LAST, LAST.of_kind("W", 3)))
            for b in range(NB):
                part = ps[:, 2 * b:2 * b + 2, :].rearrange("p a n -> p (a n)")
                step(nc.vector.tensor_tensor(y[:, b, halves[1]], part, gate_row[:, halves[1]], ALU.mult))
                if b == 1:
                    dve.wait_ge(root_done, 3)
                    nc.vector.reciprocal(stat[:, 8:9], stat[:, 6:7]).then_inc(rstd_done, 1)
                step(nc.vector.tensor_tensor(x_sb[:, b, halves[1]], x_sb[:, b, halves[1]], y[:, b, halves[1]],
                                             ALU.add))
                last_gain(b, halves[1])
                dve.wait_ge(sq_done, 2 * NB * 2 + NB + b + 1)
                nc.vector.tensor_tensor(stat[:, 4 + b:5 + b], stat[:, b:b + 1], stat[:, 2 + b:3 + b], ALU.add)\
                    .then_inc(var_done, 1)
                dve.wait_ge(var_done, 5 + 2 * b)
                nc.vector.tensor_scalar(stat[:, 4 + b:5 + b], stat[:, 4 + b:5 + b], 1.0 / D, EPS,
                                        ALU.mult, ALU.add).then_inc(var_done, 1)
            dve.wait_ge(root_done, 4)
            nc.vector.reciprocal(stat[:, 9:10], stat[:, 7:8]).then_inc(rstd_done, 1)
            dve.wait_ge(rstd_done, 4)
            dve.wait_ge(gained, 4)
            out_half = raw[:, 3, halves[0]]
            nc.vector.tensor_scalar(out_half, out_half, stat[:, 9:10], None, ALU.mult).then_inc(y_ready, 1)

        @block.tensor
        def _(pe):
            def three(dst, s_hi, s_lo, m_hi, m_lo, first, last, more=True):
                nc.tensor.matmul(dst, s_hi, m_hi, start=first, stop=False, skip_group_check=True)
                nc.tensor.matmul(dst, s_hi, m_lo, start=False, stop=False, skip_group_check=True)
                return nc.tensor.matmul(dst, s_lo, m_hi, start=False, stop=last, skip_group_check=True)

            pe.wait_ge(const_ready, 2)
            pe.wait_ge(c_act, 1)
            nc.tensor.transpose(ps[:, 7, 0:KT], c_rows[:, :], ident[0:KT, 0:KT]).then_inc(cols_ps, 1)
            pe.wait_ge(const_ready, 4)
            pe.wait_ge(rows_in, 16 * 7)
            for n in range(6):
                nc.tensor.transpose(ps[:, 6, n * 44:(n + 1) * 44], rows[0:44, n, :], ident[0:44, 0:44])
            for t in range(QT):
                mm = nc.tensor.transpose(ps[:, 6, 6 * 44 + t * 24:6 * 44 + (t + 1) * 24],
                                         b_rows[:, t * P:(t + 1) * P], ident[0:24, 0:24])
            mm.then_inc(cols_ps, 1)
            pe.wait_ge(cols_ready, 3)
            pe.sem_inc(w_used, PAIR)

            def turn_xn(n):
                bank = 0 if isinstance(n, int) and n >= NQ else 5
                pe.wait_ge(xn_ready, n + 1)
                if later(n):
                    pe.wait_ge(h_ready, n)
                for t in range(QT):
                    for b in range(NB):
                        mm = nc.tensor.transpose(ps[:, bank + t // 2, (t % 2) * S + b * P:(t % 2) * S + (b + 1) * P],
                                                 xn[:, b, t * P:(t + 1) * P], ident[:, :])
                mm.then_inc(xnT_ready, 1)

            def reduce_mods(n):
                pe.wait_ge(ada_sum, 16 * (n + 1))
                if later(n):
                    pe.wait_ge(mod_done, 3 * n)
                for half in range(2):
                    for t in range(QT):
                        mm = nc.tensor.matmul(ps[:, 7, half * QT + t:half * QT + t + 1],
                                              ada_acc[:, half, t * P:(t + 1) * P], ones[:, 0:1],
                                              start=True, stop=True, skip_group_check=True)
                mm.then_inc(mod_ps, 1)

            turn_xn(0)
            reduce_mods(0)

            def in_window(q, w):
                pe.wait_ge(win_added, q * NWIN + w + 1)
                pe.wait_ge(w_split, split(q * NWIN + w + 1))
                hi, lo = pair_hi[w % PAIR], pair_lo[w % PAIR]
                for k in range(QT):
                    for t in range(CT):
                        s = slice(k * CW + t * P, k * CW + (t + 1) * P)
                        mm = three(ps[:, 2 * (w % 2) + t // 2, (t % 2) * S:(t % 2) * S + S],
                                   hi[:, s], lo[:, s], op(op_hi, q, k), op(op_lo, q, k),
                                   k == 0 and t % 2 == 0, k == QT - 1)
                mm.then_inc(w_used, 1)

            def op(half, q, k):
                return half[:, bass.ds(q * QT + k, 1), :].rearrange("p a n -> p (a n)")

            def in_small(q):
                pe.wait_ge(ki_split, q + 1)
                for k in range(QT):
                    mm = three(ps[0:SMALL, 4, 0:S], ki_hi[:, k, :], ki_lo[:, k, :], op(op_hi, q, k), op(op_lo, q, k),
                               k == 0, k == QT - 1)
                mm.then_inc(ki_used, 1)

            def in_phase(q, more):
                pe.wait_ge(h_lo, q + 1)
                for w in range(NWIN):
                    in_window(q, w)
                    if w == 2:
                        in_small(q)
                    if w == 3 and more:
                        turn_xn(q + 1)
                    if w == 6 and more:
                        reduce_mods(q + 1)

            with pe.Fori(0, 3) as q:
                in_phase(q, True)
            in_phase(NQ - 1, False)

            pe.wait_ge(win_added, NQ * NWIN + 2)
            pe.wait_ge(ki_added, NQ)
            for b in range(NB):
                for n, t in enumerate((T_VB, T_VB + 1, T_VA, T_VA + 1)):
                    nc.tensor.transpose(ps[:, 4 + b, n * P:(n + 1) * P], proj[:, t, b * P:(b + 1) * P], ident[:, :])
            for b in range(NB):
                mm = nc.tensor.transpose(ps[:, 6, b * P:(b + 1) * P], proj[:, T_KI, b * P:(b + 1) * P], ident[:, :])
            mm.then_inc(vT_ps, 1)

            scale2_js = MID.js("Q")

            def scale2(n):
                j = scale2_js[n]
                pe.wait_ge(raw_in[MID.slot(j)], 16 * MID.loads(j))
                for m in range(NQ):
                    mm = nc.tensor.matmul(ps[32 * m:32 * m + 32, 7, :], silu_c[:, n:n + 1].to_broadcast([P, 32]),
                                          raw[:, MID.slot(j), m * CW:(m + 1) * CW],
                                          start=(n == 0), stop=(n == KT - 1), skip_group_check=True)
                mm.then_inc(q_used, 1)

            pe.wait_ge(dup_in, 16)
            for n in range(8):
                blk, hh = divmod(n, 4)
                w = P * (blk + 1)
                if n >= 2:
                    pe.wait_ge(idx_relu, n - 1)
                for odd in range(2):
                    rows_ = slice(IDXD * odd, IDXD * odd + IDXD)
                    keys = ki_dup[rows_, 0:w] if odd else proj[rows_, T_KI, 0:w]
                    for m in range(2):
                        t = T_QI + 2 * hh + m
                        mm = nc.tensor.matmul(ps[:, 2 * (n % 2) + odd, m * S:m * S + w],
                                              proj[rows_, t, blk * P:(blk + 1) * P], keys, start=True, stop=True)
                mm.then_inc(idx_ps, 1)
                if "Q" in INDEX_KINDS[n]:
                    scale2(n // 2)

            def logits(u):
                g, b = divmod(u, NB)
                w = P * (b + 1)
                if u >= 2:
                    pe.wait_ge(lg_done, u - 1)
                elif u == 0:
                    pe.wait_ge(idx_relu, 8)
                    pe.wait_ge(q_scaled, 2)
                q0, k0 = (T_QB, T_KB) if g < KV else (T_QA, T_KA)
                for r in range(4):
                    mm = nc.tensor.matmul(ps[:, 2 * (u % 2) + r // 2, (r % 2) * S:(r % 2) * S + w],
                                          proj[:, q0 + 4 * (g % KV) + r, b * P:(b + 1) * P],
                                          proj[:, k0 + g % KV, 0:w], start=True, stop=True)
                mm.then_inc(lg_ps, 1)

            def turn(u):
                pe.wait_ge(p_ready, u + 1)
                pe.wait_ge(v_ready, 2)
                if u:
                    pe.wait_ge(pT_ready, u)
                for kt in range(u % NB + 1):
                    for r in range(4):
                        mm = nc.tensor.transpose(ps[:, 4 + kt, r * P:(r + 1) * P],
                                                 logit[:, u % 2, r, kt * P:(kt + 1) * P], ident[:, :])
                mm.then_inc(pT_ps, 1)

            def values(u):
                g, b = divmod(u, NB)
                pe.wait_ge(pT_ready, u + 1)
                if u:
                    pe.wait_ge(o_lo, u)
                for kt in range(b + 1):
                    mm = nc.tensor.matmul(ps[:, 6, :], v_tok[:, kt, g, :], probT[:, kt, :],
                                          start=(kt == 0), stop=(kt == b))
                mm.then_inc(o_ps, 1)

            logits(0)
            logits(1)
            for n in range(4, 8):
                scale2(n)
            for u in range(8):
                if u < 6:
                    logits(u + 2)
                turn(u)
                scale2(8 + u)
                values(u)


            def down_chunk(seg, j, i, s_hi, s_lo, tile, bank, first, last):
                pe.wait_ge(w_split, split(seg.of_kind("W", j, i)))
                hi, lo = pair_hi[seg.pair(j)], pair_lo[seg.pair(j)]
                for k in range(2):
                    for b in range(NB):
                        tok = slice(b * P, (b + 1) * P)
                        for n, (st, w) in enumerate(((s_hi, hi), (s_hi, lo), (s_lo, hi))):
                            for a in range(2):
                                mm = nc.tensor.matmul(ps[:, bank + 2 * b + a, :], st[:, tile + k, tok],
                                                      w[:, k * 1024 + a * CW:k * 1024 + (a + 1) * CW],
                                                      start=(first and k == 0 and n == 0),
                                                      stop=(last and k == 1 and n == 2), skip_group_check=True)
                mm.then_inc(w_used, 1)

            def shift2_rows(bank):
                for m in range(NQ):
                    total = ada_acc[:, m, :] if m < 2 else y[:, 1, (m - 2) * CW:(m - 1) * CW]
                    mm = nc.tensor.matmul(ps[32 * m:32 * m + 32, bank, :], ones[:, 0:32], total,
                                          start=True, stop=True)
                mm.then_inc(rows2_ps, 1)

            def to_columns(n, bank):
                pe.wait_ge(rows2_done, n + 1)
                for t in range(QT):
                    mm = nc.tensor.transpose(ps[:, bank, t * P:(t + 1) * P], xn[:, n, t * P:(t + 1) * P],
                                             ident[:, :])
                mm.then_inc(mod2_ps, 1)

            for n, j in enumerate(MID.js("W")):
                h, pr = divmod(n, 8)
                if n == 0:
                    pe.wait_ge(o_lo, 4)
                if n == 4:
                    pe.wait_ge(o_lo, 6)
                if n == 6:
                    pe.wait_ge(o_lo, 8)
                if n == 8:
                    pe.wait_ge(gate_done, NQ)
                    pe.wait_ge(mod2_done, 1)
                down_chunk(MID, j, 0, op_hi, op_lo, 2 * MIX_PAIRS[pr], 4 * h, pr == 0, pr == 7)
                if 3 <= n < 7:
                    m = n - 3
                    pe.wait_ge(ada_sum, sums(GATE1_END))
                    if m >= 2:
                        pe.wait_ge(gate_done, m - 1)
                    nc.tensor.matmul(ps[:, GATE_BANK[m], :], ones[:, :], gate_row[:, m * CW:(m + 1) * CW],
                                     start=True, stop=True).then_inc(gate_ps, 1)
                if n == 4:
                    to_columns(0, 4)
                if n == 14:
                    pe.wait_ge(sq_done, 2 * NB + 2)
                    pe.wait_ge(ada_sum, sums(SHIFT2_END))
                    shift2_rows(0)
            to_columns(1, 1)

            def up_chunk(seg, j, i, n, inc=1):
                base = 4 if seg is UP0 else 0
                pe.wait_ge(w_split, split(seg.of_kind("W", j, i)))
                hi, lo = pair_hi[seg.pair(j)], pair_lo[seg.pair(j)]
                q = n // 2
                for k in range(QT):
                    for t in range(CT):
                        cs = slice(k * CW + t * P, k * CW + (t + 1) * P)
                        mm = three(ps[:, base + 2 * (n % 2) + t // 2, (t % 2) * S:(t % 2) * S + S],
                                   hi[:, cs], lo[:, cs], op_hi[:, q * QT + k, :], op_lo[:, q * QT + k, :],
                                   q == 0 and k == 0 and t % 2 == 0, q == NQ - 1 and k == QT - 1)
                mm.then_inc(w_used, inc)

            turn_xn(NQ)
            turn_xn(NQ + 1)
            for n in range(8):
                if n in (1, 3):
                    turn_xn(NQ + 2 + n // 2)
                pe.wait_ge(h_lo, NQ + n // 2 + 1)
                up_chunk(UP0, n, 0, n, 3 if n == 7 else 1)

            def ffn_body(seg, i, g):
                js = seg.js("W")
                for n in range(4):
                    if n == 0 and seg is not FFN_1:
                        pe.wait_ge(conv_step, 2 * CT * g)
                    if n == 1 and seg is not FFN_1:
                        pe.wait_ge(gu_done, g)
                    up_chunk(seg, js[n], i, n)
                pe.wait_ge(act_split, g)
                if seg is not FFN_1:
                    pe.wait_ge(y_added, 2 * g - 2)
                for n in range(2):
                    down_chunk(seg, js[4 + n], i, act_hi, act_lo, 2 * n, 4, n == 0, n == 1)
                for n in range(4, 8):
                    up_chunk(seg, js[2 + n], i, n)
                pe.wait_ge(y_added, 2 * g - 1)
                for n in range(2):
                    down_chunk(seg, js[10 + n], i, act_hi, act_lo, 2 * n, 4, n == 0, n == 1)

            ffn_body(FFN_1, 0, 1)
            with pe.Fori(0, FFN_A.times) as i:
                ffn_body(FFN_A, i, i + 2)
            with pe.Fori(0, FFN.times) as i:
                ffn_body(FFN, i, i + 2 + FFN_A.times)
            pe.wait_ge(ada_sum, sums(FFN.before["A"]))
            for n in range(NQ):
                if n == 0:
                    pe.wait_ge(conv_step, 2 * CT * PASSES)
                if n == 2:
                    pe.wait_ge(gu_done, PASSES)
                mm = nc.tensor.matmul(ps[:, n, :], ones[:, :], gate_row[:, n * CW:(n + 1) * CW],
                                      start=True, stop=True)
            mm.then_inc(gate2_ps, 1)
            pe.wait_ge(act_split, PASSES)
            pe.wait_ge(y_added, 2 * PASSES - 2)
            for n in range(2):
                down_chunk(LAST, n, 0, act_hi, act_lo, 2 * n, 4, n == 0, n == 1)
            pe.wait_ge(gate2_done, 1)
            for n in range(2):
                down_chunk(LAST, 2 + n, 0, act_hi, act_lo, 2 * n, 0, n == 0, n == 1)

_INS = ['x', 'c', 'w_ada', 'b_ada', 'g_mix', 'w_in', 'sinks', 'w_o', 'g_ffn', 'w_gate', 'w_up', 'conv_w',
        'conv_b', 'w_down', 'g_final']
_OUTS = [((1, S, D), 'float32')]


def kernel(**inputs):
    import numpy as _np
    import concourse.bacc as _bacc
    from concourse import mybir as _mybir
    from concourse.bass_utils import run_bass_kernel_spmd as _run

    nc = _bacc.Bacc("TRN2", target_bir_lowering=False, num_devices=1)
    arrays, args = {}, []
    for name in _INS:
        a = _np.ascontiguousarray(inputs[name])
        arrays[f"in_{name}_dram"] = a
        args.append(nc.dram_tensor(f"in_{name}_dram", a.shape, _mybir.dt.from_np(a.dtype), kind="ExternalInput").ap())
    for i, (shape, dtype) in enumerate(_OUTS):
        dt = _mybir.dt.from_np(_np.dtype(dtype))
        args.append(nc.dram_tensor(f"out_{i}_dram", shape, dt, kind="ExternalOutput").ap())
    program(nc, *args)
    r = _run(nc, [arrays], core_ids=[0])
    got = tuple(r.results[0][f"out_{i}_dram"] for i in range(len(_OUTS)))
    return got[0]
```
